# Optimizing a Trainium2 kernel written in Bass

```python
import math
import jax, jax.numpy as jnp
from jax import lax
import numpy as np

D_MODEL = 1024
BATCH = 1
SEQ = 256
DEPTH = 2

N_MIXERS = 2
N_HEADS = 8
HEAD_DIM = D_MODEL // N_HEADS
DIFF_HALF = HEAD_DIM // 2
MOBA_BLOCK = 256
MOBA_TOPK = 3
Q_BLOCK = 128
D_FF = -(-8 * D_MODEL // (3 * 256)) * 256
N_BUCKETS = 32
MAX_EXACT = N_BUCKETS // 2
MAX_DISTANCE = 2048
N_MOBA_LAYERS = (DEPTH + 1) // 2
N_DIFF_LAYERS = DEPTH // 2
RMS_EPS = 1e-6
NEG_INF = -1e30


def rms_norm(x, g):
    x32 = x.astype(jnp.float32)
    y = x32 * lax.rsqrt(jnp.mean(x32 * x32, axis=-1, keepdims=True) + RMS_EPS)
    return (y * g.astype(jnp.float32)).astype(x.dtype)

def t5_bucket(rel):
    n = jnp.maximum(rel, 0)
    nf = jnp.maximum(n, 1).astype(jnp.float32)
    large = MAX_EXACT + (jnp.log(nf / MAX_EXACT) / math.log(MAX_DISTANCE / MAX_EXACT)
                         * (N_BUCKETS - MAX_EXACT)).astype(jnp.int32)
    large = jnp.minimum(large, N_BUCKETS - 1)
    return jnp.where(n < MAX_EXACT, n, large)

def moba_attention(h, w_qkv, w_o, rel_table):
    B, S, _ = h.shape
    pad = (-S) % MOBA_BLOCK
    s_pad = S + pad
    nb = s_pad // MOBA_BLOCK
    nq = s_pad // Q_BLOCK
    k_sel_n = min(MOBA_TOPK, nb)
    q, k, v = jnp.split(h @ w_qkv, 3, axis=-1)

    def heads(t):
        t = t.reshape(B, S, N_HEADS, HEAD_DIM).transpose(0, 2, 1, 3)
        return jnp.pad(t, ((0, 0), (0, 0), (0, pad), (0, 0)))

    q = heads(q) * (HEAD_DIM ** -0.5)
    k, v = heads(k), heads(v)
    k_blk = k.reshape(B, N_HEADS, nb, MOBA_BLOCK, HEAD_DIM)
    v_blk = v.reshape(B, N_HEADS, nb, MOBA_BLOCK, HEAD_DIM)
    k_mean = jnp.mean(k_blk, axis=3)
    q_blocks = q.reshape(B, N_HEADS, nq, Q_BLOCK, HEAD_DIM).transpose(2, 0, 1, 3, 4)
    b_idx = jnp.arange(B)[:, None, None, None]
    h_idx = jnp.arange(N_HEADS)[None, :, None, None]
    table_t = rel_table.T

    def one_block(args):
        qb, qi = args
        q_pos = qi * Q_BLOCK + jnp.arange(Q_BLOCK)
        own = qi // (MOBA_BLOCK // Q_BLOCK)
        gate = jnp.einsum('bhqd,bhnd->bhqn', qb, k_mean).astype(jnp.float32)
        gate = jnp.where(jnp.arange(nb) < own, gate, NEG_INF)
        _, sel = lax.top_k(gate, k_sel_n)
        slot_valid = jnp.repeat(jnp.arange(k_sel_n) < own, MOBA_BLOCK)
        k_sel = k_blk[b_idx, h_idx, sel].reshape(B, N_HEADS, Q_BLOCK, k_sel_n * MOBA_BLOCK, HEAD_DIM)
        v_sel = v_blk[b_idx, h_idx, sel].reshape(B, N_HEADS, Q_BLOCK, k_sel_n * MOBA_BLOCK, HEAD_DIM)
        k_pos_sel = (sel[..., None] * MOBA_BLOCK + jnp.arange(MOBA_BLOCK)).reshape(
            B, N_HEADS, Q_BLOCK, k_sel_n * MOBA_BLOCK)
        bias_sel = table_t[h_idx, t5_bucket(q_pos[None, None, :, None] - k_pos_sel)]
        s_sel = jnp.einsum('bhqd,bhqkd->bhqk', qb, k_sel).astype(jnp.float32) + bias_sel.astype(jnp.float32)
        s_sel = jnp.where(slot_valid, s_sel, NEG_INF)
        k_own = lax.dynamic_slice_in_dim(k, own * MOBA_BLOCK, MOBA_BLOCK, axis=2)
        v_own = lax.dynamic_slice_in_dim(v, own * MOBA_BLOCK, MOBA_BLOCK, axis=2)
        k_pos_own = own * MOBA_BLOCK + jnp.arange(MOBA_BLOCK)
        rel_own = q_pos[:, None] - k_pos_own[None, :]
        bias_own = jnp.moveaxis(rel_table[t5_bucket(rel_own)], -1, 0)
        s_own = jnp.einsum('bhqd,bhkd->bhqk', qb, k_own).astype(jnp.float32) + bias_own[None].astype(jnp.float32)
        s_own = jnp.where(rel_own >= 0, s_own, NEG_INF)
        p = jax.nn.softmax(jnp.concatenate([s_sel, s_own], axis=-1), axis=-1).astype(v.dtype)
        n_sel = k_sel_n * MOBA_BLOCK
        return (jnp.einsum('bhqk,bhqkd->bhqd', p[..., :n_sel], v_sel)
                + jnp.einsum('bhqk,bhkd->bhqd', p[..., n_sel:], v_own))

    o = lax.map(one_block, (q_blocks, jnp.arange(nq)))
    o = o.transpose(1, 0, 3, 2, 4).reshape(B, s_pad, D_MODEL)[:, :S]
    return o @ w_o

def diff_attention(h, w_qkv, w_o, lam, subln_g, rel_table, layer_idx):
    B, S, _ = h.shape
    nq = S // Q_BLOCK
    lambda_init = 0.8 - 0.6 * math.exp(-0.3 * layer_idx)
    q, k, v = jnp.split(h @ w_qkv, 3, axis=-1)
    q = q.reshape(B, S, N_HEADS, 2, DIFF_HALF).transpose(0, 2, 3, 1, 4) * (DIFF_HALF ** -0.5)
    k = k.reshape(B, S, N_HEADS, 2, DIFF_HALF).transpose(0, 2, 3, 1, 4)
    v = v.reshape(B, S, N_HEADS, HEAD_DIM).transpose(0, 2, 1, 3)
    lam32 = lam.astype(jnp.float32)
    lam_full = (jnp.exp(jnp.sum(lam32[0] * lam32[1])) - jnp.exp(jnp.sum(lam32[2] * lam32[3]))
                + lambda_init)
    q_blocks = q.reshape(B, N_HEADS, 2, nq, Q_BLOCK, DIFF_HALF).transpose(3, 0, 1, 2, 4, 5)
    k_pos = jnp.arange(S)

    def one_block(args):
        qb, qi = args
        q_pos = qi * Q_BLOCK + jnp.arange(Q_BLOCK)
        rel = q_pos[:, None] - k_pos[None, :]
        bias = jnp.moveaxis(rel_table[t5_bucket(rel)], -1, 0)
        s = jnp.einsum('bhcqd,bhckd->bhcqk', qb, k).astype(jnp.float32) + bias[None, :, None].astype(jnp.float32)
        s = jnp.where(rel >= 0, s, NEG_INF)
        p = jax.nn.softmax(s, axis=-1)
        a = p[:, :, 0] - lam_full * p[:, :, 1]
        return jnp.einsum('bhqk,bhkd->bhqd', a.astype(v.dtype), v)

    o = lax.map(one_block, (q_blocks, jnp.arange(nq)))
    o = o.transpose(1, 2, 0, 3, 4).reshape(B, N_HEADS, S, HEAD_DIM)
    o = rms_norm(o, subln_g) * (1.0 - lambda_init)
    o = o.transpose(0, 2, 1, 3).reshape(B, S, D_MODEL)
    return o @ w_o

def swiglu(h, w_in, w_out):
    g, u = jnp.split(h @ w_in, 2, axis=-1)
    return (jax.nn.silu(g) * u) @ w_out

def first_inputs(seed: int = 0) -> dict:
    key = jax.random.key(seed)
    ks = jax.random.split(key, 16)
    f32 = jnp.float32
    D = D_MODEL
    return {
        "x": jax.random.normal(ks[0], (BATCH, SEQ, D), f32),
        "c": jax.random.normal(ks[1], (BATCH, D), f32),
        "rel_bias": 0.5 * jax.random.normal(ks[2], (N_BUCKETS, N_HEADS), f32),
        "ada_w": jax.random.normal(ks[3], (DEPTH, D, 6 * D), f32) * D ** -0.5,
        "ada_b": 0.01 * jax.random.normal(ks[4], (DEPTH, 6 * D), f32),
        "norm_g": 1.0 + 0.1 * jax.random.normal(ks[5], (DEPTH, 4, D), f32),
        "moba_w_qkv": jax.random.normal(ks[6], (N_MOBA_LAYERS, D, 3 * D), f32) * D ** -0.5,
        "moba_w_o": jax.random.normal(ks[7], (N_MOBA_LAYERS, D, D), f32) * D ** -0.5,
        "diff_w_qkv": jax.random.normal(ks[8], (N_DIFF_LAYERS, D, 3 * D), f32) * D ** -0.5,
        "diff_w_o": jax.random.normal(ks[9], (N_DIFF_LAYERS, D, D), f32) * D ** -0.5,
        "diff_lambda": 0.1 * jax.random.normal(ks[10], (N_DIFF_LAYERS, 4, DIFF_HALF), f32),
        "diff_subln_g": 1.0 + 0.1 * jax.random.normal(ks[11], (N_DIFF_LAYERS, HEAD_DIM), f32),
        "ffn_w_in": jax.random.normal(ks[12], (DEPTH, D, 2 * D_FF), f32) * D ** -0.5,
        "ffn_w_out": jax.random.normal(ks[13], (DEPTH, D_FF, D), f32) * D_FF ** -0.5,
    }

def first_block(x, c, rel_bias, ada_w, ada_b, norm_g, moba_w_qkv, moba_w_o, diff_w_qkv, diff_w_o,
              diff_lambda, diff_subln_g, ffn_w_in, ffn_w_out):
    c_act = jax.nn.silu(c)
    for i in range(DEPTH):
        mod = (c_act @ ada_w[i] + ada_b[i])[:, None, :]
        sh_a, sc_a, g_a, sh_f, sc_f, g_f = jnp.split(mod, 6, axis=-1)
        h = rms_norm(x, norm_g[i, 0]) * (1.0 + sc_a) + sh_a
        if i % N_MIXERS == 0:
            y = moba_attention(h, moba_w_qkv[i // 2], moba_w_o[i // 2], rel_bias)
        else:
            y = diff_attention(h, diff_w_qkv[i // 2], diff_w_o[i // 2], diff_lambda[i // 2],
                               diff_subln_g[i // 2], rel_bias, i)
        x = x + g_a * rms_norm(y, norm_g[i, 1])
        h = rms_norm(x, norm_g[i, 2]) * (1.0 + sc_f) + sh_f
        x = x + g_f * rms_norm(swiglu(h, ffn_w_in[i], ffn_w_out[i]), norm_g[i, 3])
    return x


DEPTH_2 = 1

D_MIX = D_MODEL
D_POOL = D_MIX // 2
D_LRU = D_MIX - D_POOL
POOL_WINDOWS = (2, 4, 8, 16)
N_POOL_GROUPS = len(POOL_WINDOWS)
POOL_GROUP_WIDTH = D_POOL // N_POOL_GROUPS
LRU_HEADS = 8
LRU_BLOCK = D_LRU // LRU_HEADS
CONV_WIDTH = 4
LRU_C = 8.0
D_FF_2 = 4 * D_MODEL
PLE_DIM = 256
D_IN_PROJ = D_POOL + D_LRU + D_LRU


def rms_norm_2(x, g):
    xf = x.astype(jnp.float32)
    y = xf * lax.rsqrt(jnp.mean(xf * xf, axis=-1, keepdims=True) + RMS_EPS)
    return (y * g.astype(jnp.float32)).astype(x.dtype)

def multiscale_pool_mixer(u, pool_w, pool_b, pool_scale):
    B, S, _ = u.shape
    ug = u.reshape(B, S, N_POOL_GROUPS, POOL_GROUP_WIDTH).astype(jnp.float32)
    csum = jnp.cumsum(ug, axis=1)
    t = jnp.arange(S)
    outs = []
    for g, w in enumerate(POOL_WINDOWS):
        c = csum[:, :, g]
        c_lag = jnp.pad(c, ((0, 0), (w, 0), (0, 0)))[:, :S]
        count = jnp.minimum(t + 1, w).astype(jnp.float32)
        outs.append((c - c_lag) / count[None, :, None] - ug[:, :, g])
    d = jnp.stack(outs, axis=2).astype(u.dtype)
    y = jnp.einsum('bsgc,gcd->bsgd', d, pool_w) + pool_b
    return y.reshape(B, S, D_POOL) * pool_scale

def causal_depthwise_conv(u, w, b):
    S = u.shape[1]
    upad = jnp.pad(u, ((0, 0), (CONV_WIDTH - 1, 0), (0, 0)))
    y = b
    for k in range(CONV_WIDTH):
        y = y + upad[:, k:k + S] * w[k]
    return y

def _linear_recurrence_combine(c1, c2):
    a1, b1 = c1
    a2, b2 = c2
    return a1 * a2, a2 * b1 + b2

def rg_lru(u, gate_a_w, gate_a_b, gate_x_w, gate_x_b, lru_L):
    B, S, W = u.shape
    uh = u.reshape(B, S, LRU_HEADS, LRU_BLOCK)
    r = jax.nn.sigmoid(jnp.einsum('bshi,hij->bshj', uh, gate_a_w) + gate_a_b).reshape(B, S, W)
    i = jax.nn.sigmoid(jnp.einsum('bshi,hij->bshj', uh, gate_x_w) + gate_x_b).reshape(B, S, W)
    log_a = LRU_C * r.astype(jnp.float32) * jax.nn.log_sigmoid(lru_L.astype(jnp.float32))
    a = jnp.exp(log_a)
    mult = jnp.sqrt(-jnp.expm1(2.0 * log_a))
    is_first = (jnp.arange(S) == 0)[None, :, None]
    mult = jnp.where(is_first, 1.0, mult)
    b = mult * (i * u).astype(jnp.float32)
    _, h = lax.associative_scan(_linear_recurrence_combine, (a, b), axis=1)
    return h.astype(u.dtype)

def second_inputs(seed: int = 0) -> dict:
    key = jax.random.key(seed)
    ks = jax.random.split(key, 24)
    f32 = jnp.float32
    nrm = lambda k, shape, scale: jax.random.normal(k, shape, f32) * scale
    gain = lambda k, shape: 1.0 + 0.05 * jax.random.normal(k, shape, f32)
    L = DEPTH_2
    rad = jnp.sqrt(jax.random.uniform(ks[12], (L, D_LRU), f32, 0.9 ** 2, 0.999 ** 2))
    lru_L = jnp.log(rad) - jnp.log1p(-rad)
    return {
        "x": jax.random.normal(ks[0], (BATCH, SEQ, D_MODEL), f32),
        "p": jax.random.normal(ks[1], (DEPTH_2, BATCH, SEQ, PLE_DIM), f32),
        "norm_mix_g": gain(ks[2], (L, D_MODEL)),
        "w_in": nrm(ks[3], (L, D_MODEL, D_IN_PROJ), D_MODEL ** -0.5),
        "pool_w": nrm(ks[4], (L, N_POOL_GROUPS, POOL_GROUP_WIDTH, POOL_GROUP_WIDTH), POOL_GROUP_WIDTH ** -0.5),
        "pool_b": nrm(ks[5], (L, N_POOL_GROUPS, POOL_GROUP_WIDTH), 0.01),
        "pool_scale": gain(ks[6], (L, D_POOL)),
        "conv_w": nrm(ks[7], (L, CONV_WIDTH, D_LRU), CONV_WIDTH ** -0.5),
        "conv_b": nrm(ks[8], (L, D_LRU), 0.01),
        "gate_a_w": nrm(ks[9], (L, LRU_HEADS, LRU_BLOCK, LRU_BLOCK), LRU_BLOCK ** -0.5),
        "gate_a_b": nrm(ks[10], (L, LRU_HEADS, LRU_BLOCK), 0.01),
        "gate_x_w": nrm(ks[11], (L, LRU_HEADS, LRU_BLOCK, LRU_BLOCK), LRU_BLOCK ** -0.5),
        "gate_x_b": nrm(ks[13], (L, LRU_HEADS, LRU_BLOCK), 0.01),
        "lru_L": lru_L,
        "w_out": nrm(ks[14], (L, D_MIX, D_MODEL), D_MIX ** -0.5),
        "norm_mlp_g": gain(ks[15], (L, D_MODEL)),
        "w_up": nrm(ks[16], (L, D_MODEL, D_FF_2), D_MODEL ** -0.5),
        "w_down": nrm(ks[17], (L, D_FF_2, D_MODEL), D_FF_2 ** -0.5),
        "norm_ple_g": gain(ks[18], (L, D_MODEL)),
        "w_ple_gate": nrm(ks[19], (L, D_MODEL, D_MODEL), D_MODEL ** -0.5),
        "b_ple_gate": nrm(ks[20], (L, D_MODEL), 0.01),
        "w_ple_proj": nrm(ks[21], (L, PLE_DIM, D_MODEL), PLE_DIM ** -0.5),
        "norm_final_g": gain(ks[22], (D_MODEL,)),
    }

def second_block(x, p, norm_mix_g, w_in, pool_w, pool_b, pool_scale, conv_w, conv_b,
              gate_a_w, gate_a_b, gate_x_w, gate_x_b, lru_L, w_out, norm_mlp_g,
              w_up, w_down, norm_ple_g, w_ple_gate, b_ple_gate, w_ple_proj, norm_final_g):
    h = x
    for l in range(DEPTH_2):
        z = rms_norm_2(h, norm_mix_g[l])
        proj = z @ w_in[l]
        u_pool = proj[..., :D_POOL]
        u_lru = proj[..., D_POOL:D_POOL + D_LRU]
        u_gate = proj[..., D_POOL + D_LRU:]
        y_pool = multiscale_pool_mixer(u_pool, pool_w[l], pool_b[l], pool_scale[l])
        xb = causal_depthwise_conv(u_lru, conv_w[l], conv_b[l])
        y_lru = rg_lru(xb, gate_a_w[l], gate_a_b[l], gate_x_w[l], gate_x_b[l], lru_L[l])
        y_lru = y_lru * jax.nn.gelu(u_gate)
        h = h + jnp.concatenate([y_pool, y_lru], axis=-1) @ w_out[l]
        z = rms_norm_2(h, norm_mlp_g[l])
        h = h + jnp.square(jax.nn.relu(z @ w_up[l])) @ w_down[l]
        z = rms_norm_2(h, norm_ple_g[l])
        gate = jax.nn.sigmoid(z @ w_ple_gate[l] + b_ple_gate[l])
        h = h + gate * (p[l] @ w_ple_proj[l])
    return rms_norm_2(h, norm_final_g)


def setup_inputs(seed=0):
    out = dict(first_inputs(seed))
    for name, value in second_inputs(seed + 1).items():
        if name != "x":
            out[name + "_2"] = value
    return out


def reference(
    x, c, rel_bias, ada_w, ada_b, norm_g, moba_w_qkv, moba_w_o, diff_w_qkv, diff_w_o,
    diff_lambda, diff_subln_g, ffn_w_in, ffn_w_out, p_2, norm_mix_g_2, w_in_2, pool_w_2,
    pool_b_2, pool_scale_2, conv_w_2, conv_b_2, gate_a_w_2, gate_a_b_2, gate_x_w_2, gate_x_b_2,
    lru_L_2, w_out_2, norm_mlp_g_2, w_up_2, w_down_2, norm_ple_g_2, w_ple_gate_2, b_ple_gate_2,
    w_ple_proj_2, norm_final_g_2,
):
    x = first_block(
        x, c, rel_bias, ada_w, ada_b, norm_g, moba_w_qkv, moba_w_o, diff_w_qkv, diff_w_o,
        diff_lambda, diff_subln_g, ffn_w_in, ffn_w_out,
    )
    return second_block(
        x, p_2, norm_mix_g_2, w_in_2, pool_w_2, pool_b_2, pool_scale_2, conv_w_2, conv_b_2,
        gate_a_w_2, gate_a_b_2, gate_x_w_2, gate_x_b_2, lru_L_2, w_out_2, norm_mlp_g_2, w_up_2,
        w_down_2, norm_ple_g_2, w_ple_gate_2, b_ple_gate_2, w_ple_proj_2, norm_final_g_2,
    )


_drawn_inputs = setup_inputs


def setup_inputs(seed=0):
    import zlib

    import numpy as np

    out = dict(_drawn_inputs(seed))
    spreads = {}
    factors = {'pool_b_2': 8.0,
     'pool_scale_2': 3.873,
     'conv_b_2': 8.0,
     'gate_a_b_2': 64.0,
     'gate_x_b_2': 64.0,
     'norm_ple_g_2': 36.693,
     'b_ple_gate_2': 200.0}
    for name, (base, spread) in spreads.items():
        noise = np.random.default_rng([zlib.crc32(name.encode()), seed]).standard_normal(out[name].shape)
        drawn = base * np.exp(spread * noise) if base else spread * noise
        out[name] = __import__('jax').numpy.asarray(drawn.astype(out[name].dtype))
    for name, factor in factors.items():
        out[name] = (out[name] * factor).astype(out[name].dtype)
    return out
```

```python
import math
from contextlib import ExitStack

import numpy as np
import concourse.bass as bass
from concourse import mybir

F32 = mybir.dt.float32
F32R = mybir.dt.float32r
BF16 = mybir.dt.bfloat16
ACT = mybir.ActivationFunctionType
ALU = mybir.AluOpType
AX_X = mybir.AxisListType.X

P = 128
D = 1024
KT = D // P
S = 256
ST = S // P
DEPTH = 2
HEADS = 8
HD = D // HEADS
HALF = HD // 2
D_FF = -(-8 * D // (3 * 256)) * 256
N_BUCKETS = 32
MAX_EXACT = N_BUCKETS // 2
MAX_DISTANCE = 2048
EPS = 1e-6
NEG_INF = -1e30
LAMBDA_INIT = 0.8 - 0.6 * math.exp(-0.3 * 1)
D_MIX_HALF = D // 2
CT = D_MIX_HALF // P
POOL_WINDOWS = (2, 4, 8, 16)
MAX_WINDOW = max(POOL_WINDOWS)
CONV = 4
LRU_C = 8.0
LRU_BLOCK = 64
D_FF_2 = 4 * D
PLE = 256

RING = 3
SLAB = 2048
PAIRS = HEADS // 2
FF_CHUNKS = D_FF // 256
UP_CHUNKS = D_FF_2 // 256

PER_LAYER = 3 * PAIRS + KT // 2 + 3 * FF_CHUNKS
ATTN = [l * PER_LAYER for l in range(DEPTH)]
OPROJ = [a + 3 * PAIRS for a in ATTN]
FFN = [o + KT // 2 for o in OPROJ]
MIX_IN = DEPTH * PER_LAYER
MIX_OUT = MIX_IN + 6
MLP = MIX_OUT + 4
PLE_PROJ = MLP + 2 * UP_CHUNKS
PLE_GATE = PLE_PROJ + 1
N_SLABS = PLE_GATE + 4

SH_A, SC_A, G_A, SH_F, SC_F, G_F = range(6)
ADA_RING = 3

FLIP_BANKS = [4, 5, 6, 7, 3, 2]
MISC = 3
FF_ACC = [4, 5, 6, 7]
OP_ACC = [0, 1, 2, 7]

ROW_C = 6 * DEPTH * KT
R_NORM, R_MIX, R_MLP, R_PLE, R_FINAL, R_PLE_B, R_CONV_W, R_CONV_B, R_GA_B = 0, 64, 72, 80, 88, 96, 104, 120, 124
N_VECTORS = 14
N_LATE = 6
LRUC_STEPS = 17
R_GX_B, R_L, R_POOL_B, R_POOL_S, R_SUBLN = 0, 4, 8, 12, 16


class Slab:

    def __init__(self, first, stride=0, i=0):
        self.first, self.stride, self.i = first, stride, i

    def __add__(self, k):
        return Slab(self.first + k, self.stride, self.i)

    @property
    def place(self):
        return self.first % RING

    @property
    def turn(self):
        return self.first // RING + (self.stride // RING) * self.i if self.stride else self.first // RING

    def plus(self, k):
        return self.first + k + self.stride * self.i if self.stride else self.first + k


def bucket(n):
    if n < MAX_EXACT:
        return n
    f = np.float32
    large = MAX_EXACT + int(np.log(f(n) / f(MAX_EXACT)) / f(math.log(MAX_DISTANCE / MAX_EXACT))
                            * f(N_BUCKETS - MAX_EXACT))
    return min(large, N_BUCKETS - 1)


def bucket_runs():
    runs, j = [], 0
    while j < S:
        b, e = bucket(S - 1 - j), j
        while e < S and bucket(S - 1 - e) == b:
            e += 1
        runs.append((j, e, b))
        j = e
    return runs


def build(nc, x, c, rel_bias, ada_w, ada_b, norm_g, moba_w_qkv, moba_w_o, diff_w_qkv, diff_w_o, diff_lambda,
          diff_subln_g, ffn_w_in, ffn_w_out, p_2, norm_mix_g_2, w_in_2, pool_w_2, pool_b_2, pool_scale_2,
          conv_w_2, conv_b_2, gate_a_w_2, gate_a_b_2, gate_x_w_2, gate_x_b_2, lru_L_2, w_out_2, norm_mlp_g_2,
          w_up_2, w_down_2, norm_ple_g_2, w_ple_gate_2, b_ple_gate_2, w_ple_proj_2, norm_final_g_2, out):
    V, A, T, G = nc.vector, nc.scalar, nc.tensor, nc.gpsimd
    ds = bass.ds
    LINE = 3 * P
    line_dram = nc.dram_tensor("bias_line", (HEADS, LINE), F32, kind="Internal").ap()

    with ExitStack() as ctx:
        def sb(name, shape, dt=F32):
            return ctx.enter_context(nc.sbuf_tensor(name, shape, dt))

        def sem(name):
            return ctx.enter_context(nc.semaphore(name))

        raw = sb("raw", [P, RING, SLAB])
        w_hi = sb("w_hi", [P, RING, SLAB], F32R)
        w_lo = sb("w_lo", [P, RING, SLAB], F32R)
        ada_raw = sb("ada_raw", [P, ADA_RING, 2, D])
        ada_sum = sb("ada_sum", [P, 3, D])
        xt = sb("xt", [P, KT, S])
        y = sb("y", [P, KT, S])
        sq = sb("sq", [P, 2, 2, S])
        h_hi = sb("h_hi", [P, KT, S], F32R)
        h_lo = sb("h_lo", [P, KT, S], F32R)
        o_hi = sb("o_hi", [P, KT, S], F32R)
        o_lo = sb("o_lo", [P, KT, S], F32R)
        silu_g = sb("silu_g", [P, 2, S])
        hid = sb("hid", [P, 2, S])
        hid_hi = sb("hid_hi", [P, 2, S], F32R)
        hid_lo = sb("hid_lo", [P, 2, S], F32R)
        qkv = sb("qkv", [P, 3, 2, S])
        bias = sb("bias", [P, HEADS, LINE])
        prob = sb("prob", [P, 4, LINE])
        pt = sb("pt", [P, 2, LINE])
        tabA = sb("tabA", [P, P])
        tabB = sb("tabB", [P, P])
        tabC = sb("tabC", [P, 32])
        ident = sb("ident", [P, P])
        flip = sb("flip", [P, P])
        ones = sb("ones", [P, P])
        zeros = sb("zeros", [P, 512], BF16)
        c_act = sb("c_act", [P, KT])
        c_pair = sb("c_pair", [P, 2])
        mods = sb("mods", [P, 12, KT])
        gain = sb("gain", [P, 4 * DEPTH, KT])
        rms = sb("rms", [P, S])
        rstd = sb("rstd", [P, S])
        maxes = sb("maxes", [P, 2, 4])
        sums = sb("sums", [P, 2, 4])
        rsums = sb("rsums", [P, 2, 4])
        eps = sb("eps", [P, 1])
        lam_in = sb("lam_in", [P, 4, HALF])
        lam_prod = sb("lam_prod", [P, 2, HALF])
        lam_s = sb("lam_s", [P, 4])
        neg_lam = sb("neg_lam", [P, 1])
        subln = sb("subln", [P, 1])
        rel_rows = sb("rel_rows", [N_BUCKETS, HEADS])
        rel_t = sb("rel_t", [HEADS, N_BUCKETS])
        line = sb("line", [HEADS, LINE])
        inv_t = sb("inv_t", [P, MAX_WINDOW])
        lruc = sb("lruc", [P, 8, CT])

        rowsA, rowsB, rowsC = (hid[:].rearrange("p a b -> p (a b)")[:, n * P:(n + 1) * P] for n in range(3))

        small_w = qkv[:].rearrange("p a b c -> p (a b c)").rearrange("p (g t d) -> p g t d", g=3, t=CT)
        p_in = pt[:, :, 0:PLE]
        PADC = CONV - 1
        ul = prob[:].rearrange("p a b -> p (a b)")[:, 0:CT * (PADC + S)].rearrange("p (t s) -> p t s", t=CT)
        flat = ada_raw[:].rearrange("p a b c -> p (a b c)")
        view = lambda n: flat[:, n * CT * S:(n + 1) * CT * S].rearrange("p (t s) -> p t s", t=CT)
        xb, gate_r, gate_i, a_t, th, mult = (view(n) for n in range(6))
        bias_flat = bias[:].rearrange("p a b -> p (a b)")
        bflat = bias[:].rearrange("p a b -> p (a b)")
        lru_h = bflat[:, 0:CT * S].rearrange("p (t s) -> p t s", t=CT)
        gelu_t = bflat[:, CT * S:2 * CT * S].rearrange("p (t s) -> p t s", t=CT)
        pool_d = bflat[:, 2 * CT * S:3 * CT * S].rearrange("p (t s) -> p t s", t=CT)
        PADW = MAX_WINDOW
        asum = ada_sum[:].rearrange("p a b -> p (a b)")
        win = [asum[:, n * 1280:n * 1280 + CT * (PADW + S)].rearrange("p (t s) -> p t s", t=CT) for n in range(2)]
        up = y[:].rearrange("p a b -> p (a b)")[:, 0:CT * (PADW + S)].rearrange("p (t s) -> p t s", t=CT)
        proj = bias[:].rearrange("p a b -> p (a b)")[:, 0:KT * S].rearrange("p (t s) -> p t s", t=KT)
        gate = silu_g
        out_tok = ada_raw[:, 0]
        x_tok = y[:].rearrange("p a b -> p (a b)").rearrange("p (t d) -> p t d", t=ST)

        ps = ctx.enter_context(nc.psum_tensor("ps", [P, 8, 512], F32))

        def acc(banks, t):
            return ps[:, banks[t // 2], (t % 2) * S:(t % 2) * S + S]

        slab_loaded = [sem(f"slab_loaded_{i}") for i in range(RING)]
        slab_hi, slab_lo, slab_done = sem("slab_hi"), sem("slab_lo"), sem("slab_done")
        ada_loaded = [sem(f"ada_loaded_{i}") for i in range(ADA_RING)]
        ada_acc, ada_zero, ada_reduced, mod_ready, gain_ready = (
            sem(n) for n in ("ada_acc", "ada_zero", "ada_reduced", "mod_ready", "gain_ready"))
        c_pair_ready = sem("c_pair_ready")
        rows_loaded, small_loaded, x_loaded = sem("rows_loaded"), sem("small_loaded"), sem("x_loaded")
        rowsA_loaded = sem("rowsA_loaded")
        ident_step, const_ready, diag_zero = sem("ident_step"), sem("const_ready"), sem("diag_zero")
        tab_turned, tab_ready, c_ready = sem("tab_turned"), sem("tab_ready"), sem("c_ready")
        rel_turned, rel_ready, line_zero, line_ready, line_stored, bias_loaded = (
            sem(n) for n in ("rel_turned", "rel_ready", "line_zero", "line_ready", "line_stored", "bias_loaded"))
        x_turned, x_ready = sem("x_turned"), sem("x_ready")
        sq_ready, sq_used, sum_done, rms_ready, rstd_ready = (
            sem(n) for n in ("sq_ready", "sq_used", "sum_done", "rms_ready", "rstd_ready"))
        h_norm, h_hi_ready, h_ready = sem("h_norm"), sem("h_hi_ready"), sem("h_ready")
        acc_done, y_copied, y_scaled = sem("acc_done"), sem("y_copied"), sem("y_scaled")
        qkv_out, s_done, s_biased, s_max, s_negmax, s_exp, s_rsum, s_mixed, p_ready = (
            sem(n) for n in ("qkv_out", "s_done", "s_biased", "s_max", "s_negmax", "s_exp", "s_rsum",
                             "s_mixed", "p_ready"))
        pt_done, pt_act, pt_dve, pv_done, o_hi_ready, o_ready = (
            sem(n) for n in ("pt_done", "pt_act", "pt_dve", "pv_done", "o_hi_ready", "o_ready"))
        head_copied, head_sq, head_sum, head_rms, head_rstd, head_norm = (
            sem(n) for n in ("head_copied", "head_sq", "head_sum", "head_rms", "head_rstd", "head_norm"))
        silu_ready, hid_ready, hid_hi_ready, hid_lo_ready, acc_cleared = (
            sem(n) for n in ("silu_ready", "hid_ready", "hid_hi_ready", "hid_lo_ready", "acc_cleared"))
        relu_ready = sem("relu_ready")
        lam_step, lam_exp = sem("lam_step"), sem("lam_exp")
        lruc_exp, lruc_step = sem("lruc_exp"), sem("lruc_step")
        mix_out, conv_step, conv_done, gates_done, gates_out, lru_exp, lru_step, lru_mult, lru_scan = (
            sem(n) for n in ("mix_out", "conv_step", "conv_done", "gates_done", "gates_out", "lru_exp",
                             "lru_step", "lru_mult", "lru_scan"))
        pads_zero, pool_step, pool_done, pool_mm, pool_out, gelu_ready, lru_ready = (
            sem(n) for n in ("pads_zero", "pool_step", "pool_done", "pool_mm", "pool_out", "gelu_ready",
                             "lru_ready"))
        mix_hi, mix_ready = sem("mix_hi"), sem("mix_ready")
        p_turned, p_hi_ready, p_lo_ready = (sem(n) for n in ("p_turned", "p_hi_ready", "p_lo_ready"))
        proj_done, proj_out, gate_out, gate_mixed = (
            sem(n) for n in ("proj_done", "proj_out", "gate_out", "gate_mixed"))
        final_ready, final_turned, final_out, stored = (
            sem(n) for n in ("final_ready", "final_turned", "final_out", "stored"))
        out_act, out_dve, lru_in, inv_ready, rel_loaded, late_loaded = (
            sem(n) for n in ("out_act", "out_dve", "lru_in", "inv_ready", "rel_loaded", "late_loaded"))
        lam_loaded, bias_turned, bias_ready = sem("lam_loaded"), sem("bias_turned"), sem("bias_ready")

        def cols(w, start):
            return w.rearrange("(k p) n -> p k n", p=P)[:, :, ds(start, 256)]

        def rows(w, j):
            return w.rearrange("(j k p) n -> p j k n", p=P, k=2)[:, ds(j, 1)].rearrange("p j k n -> p (j k) n")

        w_qkv = [moba_w_qkv[0], diff_w_qkv[0]]
        w_o = [moba_w_o[0], diff_w_o[0]]
        as_cols = lambda t: t.rearrange("p (k n) -> p k n", k=KT)
        as_rows = lambda t: t.rearrange("p (k n) -> p k n", k=2)

        def row_tiles(v):
            return v.rearrange("(t p) -> t p", p=P)

        block = ctx.enter_context(nc.Block())

        @block.sync
        def _(sp):
            def load(n, src, by_rows):
                if n.stride or n.first >= RING:
                    sp.wait_ge(slab_lo, n.plus(1 - RING))
                place = raw[:, n.place]
                sp.dma_start(as_rows(place) if by_rows else as_cols(place), src)\
                    .then_inc(slab_loaded[n.place], 16)

            sp.dma_start(rowsA[0:ROW_C, :], ada_b.rearrange("l (t p) -> (l t) p", p=P)).then_inc(rowsA_loaded, 16)
            sp.dma_start(rowsA[ROW_C:ROW_C + KT, :], row_tiles(c[0])).then_inc(rowsA_loaded, 16)
            sp.dma_start(rel_rows[:], rel_bias).then_inc(rel_loaded, 16)
            sp.dma_start(x_tok, x[0].rearrange("(t p) d -> p t d", p=P)).then_inc(x_loaded, 16)
            vectors = (
                (rowsB, R_NORM, 4 * DEPTH * KT, norm_g.rearrange("l n (t p) -> (l n t) p", p=P)),
                (rowsB, R_MIX, KT, row_tiles(norm_mix_g_2[0])), (rowsB, R_MLP, KT, row_tiles(norm_mlp_g_2[0])),
                (rowsB, R_PLE, KT, row_tiles(norm_ple_g_2[0])), (rowsB, R_FINAL, KT, row_tiles(norm_final_g_2)),
                (rowsB, R_PLE_B, KT, row_tiles(b_ple_gate_2[0])),
                (rowsB, R_CONV_W, CONV * CT, conv_w_2[0].rearrange("k (t p) -> (k t) p", p=P)),
                (rowsB, R_CONV_B, CT, row_tiles(conv_b_2[0])),
                (rowsB, R_GA_B, CT, gate_a_b_2[0].rearrange("(t h) d -> t (h d)", h=2)),
                (rowsC, R_GX_B, CT, gate_x_b_2[0].rearrange("(t h) d -> t (h d)", h=2)),
                (rowsC, R_L, CT, row_tiles(lru_L_2[0])), (rowsC, R_POOL_B, CT, pool_b_2[0]),
                (rowsC, R_POOL_S, CT, row_tiles(pool_scale_2[0])), (rowsC, R_SUBLN, 1, diff_subln_g),
            )
            assert len(vectors) == N_VECTORS
            for dst, r, n, src in vectors:
                sp.dma_start(dst[r:r + n, :], src).then_inc(rows_loaded, 16)
            sp.wait_ge(ada_loaded[2], 16 * 2)
            for l in range(DEPTH):
                for t in range(3):
                    load(Slab(ATTN[l] + t), cols(w_qkv[l], t * D), False)
                with sp.Fori(1, PAIRS) as j:
                    for t in range(3):
                        load(Slab(ATTN[l] + t, 3, j), cols(w_qkv[l], j * 256 + t * D), False)
                for j in range(KT // 2):
                    load(Slab(OPROJ[l] + j), rows(w_o[l], j), True)
                load(Slab(FFN[l]), cols(ffn_w_in[l], 0), False)
                load(Slab(FFN[l] + 1), cols(ffn_w_in[l], D_FF), False)
                with sp.Fori(0, FF_CHUNKS - 1) as j:
                    n = Slab(FFN[l] + 2, 3, j)
                    load(n, cols(ffn_w_in[l], j * 256 + 256), False)
                    load(n + 1, cols(ffn_w_in[l], j * 256 + (D_FF + 256)), False)
                    load(n + 2, rows(ffn_w_out[l], j), True)
                load(Slab(FFN[l] + 3 * FF_CHUNKS - 1), rows(ffn_w_out[l], FF_CHUNKS - 1), True)
                if l == 0:
                    sp.dma_start(lam_in[:], bass.AP(diff_lambda.tensor, 0, [[0, P], [HALF, 4], [1, HALF]]))\
                        .then_inc(lam_loaded, 16)
            sp.wait_ge(diag_zero, 1)
            late = [(p_in, p_2[0, 0].rearrange("(t p) d -> p t d", p=P)),
                    (small_w[:, 2], pool_w_2[0].rearrange("g c d -> c g d"))]
            for g, w in enumerate((gate_a_w_2, gate_x_w_2)):
                for hh in range(2):
                    at = slice(hh * LRU_BLOCK, (hh + 1) * LRU_BLOCK)
                    late.append((small_w[at, g, :, at], w[0].rearrange("(t h) i j -> h i t j", h=2)[hh]))
            assert len(late) == N_LATE
            for dst, src in late:
                sp.dma_start(dst, src).then_inc(late_loaded, 16)
            for s, col in enumerate((512, 768, 0, 256, 1024, 1280)):
                load(Slab(MIX_IN + s), cols(w_in_2[0], col), False)
            for j in range(KT // 2):
                load(Slab(MIX_OUT + j), rows(w_out_2[0], j), True)
            load(Slab(MLP), cols(w_up_2[0], 0), False)
            with sp.Fori(0, (UP_CHUNKS - 1) // 3) as i:
                for c3 in range(3):
                    n = Slab(MLP + 1 + 2 * c3, 6, i)
                    load(n, cols(w_up_2[0], i * 768 + 256 * (c3 + 1)), False)
                    load(n + 1, rows(w_down_2[0], i * 3 + c3), True)
            load(Slab(MLP + 2 * UP_CHUNKS - 1), rows(w_down_2[0], UP_CHUNKS - 1), True)
            load(Slab(PLE_PROJ), rows(w_ple_proj_2[0], 0), True)
            for j in range(4):
                load(Slab(PLE_GATE + j), cols(w_ple_gate_2[0], 256 * j), False)
            for t in range(ST):
                sp.wait_ge(out_act, t + 1)
                sp.wait_ge(out_dve, t + 1)
                sp.dma_start(out[0, t * P:(t + 1) * P, :], out_tok[:, t]).then_inc(stored, 16)
            sp.wait_ge(stored, 16 * ST)

        @block.gpsimd
        def _(pool):
            def load_ada(l, kp, col, place, need):
                if need is not None:
                    pool.wait_ge(ada_acc, need)
                pool.dma_start(ada_raw[:, place], rows(ada_w[l][:, ds(col, D)], kp)).then_inc(ada_loaded[place], 16)

            for m in range(3):
                load_ada(0, m % 4, 0, (m + 1) % 3, None)
            G.memset(ident[:], 0.0).then_inc(ident_step, 1)
            pool.wait_ge(ident_step, 1)
            G.affine_select(out=ident[:], in_=ident[:], compare_op=ALU.not_equal, fill=1.0, base=0,
                            pattern=[[-1, P]], channel_multiplier=1).then_inc(ident_step, 1)
            G.memset(flip[:], 0.0).then_inc(ident_step, 1)
            pool.wait_ge(ident_step, 3)
            G.affine_select(out=flip[:], in_=flip[:], compare_op=ALU.not_equal, fill=1.0, base=1 - P,
                            pattern=[[1, P]], channel_multiplier=1).then_inc(ident_step, 1)
            G.memset(line[:], NEG_INF).then_inc(line_zero, 1)
            for m in range(3, 8):
                load_ada(0, m % 4, (m // 4) * D, (m + 1) % 3, 2 * (m - 2))
            pool.wait_ge(line_zero, 1)
            pool.wait_ge(rel_ready, 1)
            for a, b, k in bucket_runs():
                last = G.tensor_copy(line[:, a:b], rel_t[:, k:k + 1].to_broadcast([HEADS, b - a]))
            last.then_inc(line_ready, 1)
            pool.wait_ge(line_ready, 1)
            pool.dma_start(line_dram, line[:]).then_inc(line_stored, 16)
            pool.wait_ge(line_stored, 16)
            for first, at, width in ((0, 0, S), (P, S, P)):
                src = bass.AP(line_dram.tensor, first, [[1, P], [LINE, HEADS], [1, width]])
                pool.dma_start(bias[:, :, at:at + width], src).then_inc(bias_loaded, 16)
            for t in range(MAX_WINDOW):
                last = G.memset(inv_t[:, t:t + 1], 1.0 / (t + 1))
            last.then_inc(inv_ready, 1)
            with pool.Fori(0, PAIRS) as j:
                for c3 in range(3):
                    load_ada(0, j, (G_A + c3) * D, c3, j * 6 + 2 * (8 + c3 - 2))
            for m in range(20, 24):
                load_ada(0, m % 4, G_F * D, (m + 1) % 3, 2 * (m - 2))
            with pool.Fori(0, 5) as i:
                for kp in range(4):
                    load_ada(1, kp, i * D, (kp + 1) % 2, i * 8 + 2 * (24 + kp - 1))
            with pool.Fori(0, PAIRS) as j:
                load_ada(1, j, G_F * D, 2, j * 2 + 2 * 44)
            pool.wait_ge(o_ready, DEPTH * PAIRS)
            G.memset(qkv[:], 0.0).then_inc(diag_zero, 1)

        @block.tensor
        def _(pe):
            def three(out_ap, hi_s, lo_s, hi_m, lo_m, start, stop):
                T.matmul(out_ap, hi_s, hi_m, start=start, stop=False, skip_group_check=True)
                T.matmul(out_ap, hi_s, lo_m, start=False, stop=False, skip_group_check=True)
                return T.matmul(out_ap, lo_s, hi_m, start=False, stop=stop, skip_group_check=True)

            def col_slab(n, h_base=None):
                pe.wait_ge(slab_lo, n.plus(1))
                wh, wl = as_cols(w_hi[:, n.place]), as_cols(w_lo[:, n.place])
                for k in range(KT):
                    if h_base is not None:
                        pe.wait_ge(h_ready, h_base + k + 1)
                    for o in range(2):
                        cs = slice(o * P, o * P + P)
                        last = three(ps[:, n.place, o * S:(o + 1) * S], wh[:, k, cs], wl[:, k, cs],
                                     h_hi[:, k], h_lo[:, k], k == 0 and o == 0, k == KT - 1)
                last.then_inc(slab_done, 1)

            def v_slab(n):
                pe.wait_ge(slab_lo, n.plus(1))
                wh, wl = as_cols(w_hi[:, n.place]), as_cols(w_lo[:, n.place])
                for k in range(KT):
                    for t in range(ST):
                        ts = slice(t * P, t * P + P)
                        last = three(ps[:, n.place, t * 256:(t + 1) * 256], h_hi[:, k, ts], h_lo[:, k, ts],
                                     wh[:, k], wl[:, k], k == 0 and t == 0, k == KT - 1)
                last.then_inc(slab_done, 1)

            def row_slab(n, banks, hi, lo, first, final):
                pe.wait_ge(slab_lo, n.plus(1))
                wh, wl = as_rows(w_hi[:, n.place]), as_rows(w_lo[:, n.place])
                for t in range(KT):
                    cs = slice(t * P, t * P + P)
                    for k in range(2):
                        last = three(acc(banks, t), wh[:, k, cs], wl[:, k, cs], hi[:, k], lo[:, k],
                                     first and k == 0 and t % 2 == 0, final and k == 1)
                    if final and t % 2 == 1 and t < KT - 1:
                        last.then_inc(acc_done, 1)
                last.then_inc(slab_done, 1)

            def sum_squares(norm):
                for b in range(KT // 2):
                    pe.wait_ge(sq_ready, 4 * norm + b + 1)
                    for o in range(2):
                        last = T.matmul(ps[:, MISC, 0:S], ones[:], sq[:, b % 2, o], start=b == 0 and o == 0,
                                        stop=b == 3 and o == 1)
                    last.then_inc(sq_used, 1)

            def reduce_mods(bank, slots):
                for s in range(slots):
                    for t in range(KT):
                        last = T.matmul(ps[:, bank, s * KT + t:s * KT + t + 1], ada_sum[:, s, t * P:(t + 1) * P],
                                        ones[:, 0:1], start=True, stop=True)
                last.then_inc(ada_reduced, 1)

            def clear_acc(banks):
                for b in banks:
                    T.matmul(ps[:, b], zeros[:, 0:P], zeros[:], start=True, stop=True, skip_group_check=True)

            pe.wait_ge(ident_step, 2)
            pe.wait_ge(rowsA_loaded, 32)
            T.transpose(ps[:, 0, 0:ROW_C + KT], rowsA[0:ROW_C + KT, :], ident[0:ROW_C + KT, 0:ROW_C + KT])\
                .then_inc(tab_turned, 1)
            pe.wait_ge(rel_loaded, 16)
            T.transpose(ps[0:HEADS, 1, 0:N_BUCKETS], rel_rows[:], ident[0:N_BUCKETS, 0:N_BUCKETS])\
                .then_inc(rel_turned, 1)
            pe.wait_ge(x_loaded, 16)
            for b in range(4):
                for o in range(2):
                    for t in range(ST):
                        f = 2 * b + o
                        last = T.transpose(ps[:, 4 + b, o * S + t * P:o * S + (t + 1) * P],
                                           x_tok[:, t, f * P:(f + 1) * P], ident[:])
                last.then_inc(x_turned, 1)
            pe.wait_ge(rows_loaded, 16 * N_VECTORS)
            T.transpose(ps[:, 2, 0:P], rowsB, ident[:]).then_inc(tab_turned, 1)
            pe.wait_ge(tab_ready, 1)
            T.transpose(ps[:, 0, 0:R_SUBLN + 1], rowsC[0:R_SUBLN + 1, :], ident[0:R_SUBLN + 1, 0:R_SUBLN + 1])\
                .then_inc(tab_turned, 1)
            pe.wait_ge(const_ready, 3)
            sum_squares(0)
            pe.wait_ge(ada_acc, 2 * 8)
            pe.wait_ge(rel_ready, 1)
            reduce_mods(1, 2)
            pe.wait_ge(ident_step, 4)
            pe.wait_ge(bias_loaded, 32)
            pe.wait_ge(x_ready, 4)
            pe.wait_ge(rms_ready, 1)
            for b, bank in enumerate(FLIP_BANKS):
                T.matmul(ps[:, bank], flip[:], bias_flat[:, b * 512:(b + 1) * 512], start=True, stop=True)\
                    .then_inc(bias_turned, 1)

            for l in range(DEPTH):
                units = 1 + l

                def turn_probs(pairs):
                    pe.wait_ge(p_ready, pairs)
                    for hh in range(2):
                        u, b = hh * units, 5 + hh
                        T.transpose(ps[:, b, 0:P], prob[:, u, S:S + P], ident[:])
                        T.transpose(ps[:, b, P:2 * P], prob[:, u, 0:P], ident[:])
                        T.transpose(ps[:, b, 2 * P:3 * P], prob[:, u, P:2 * P], ident[:]).then_inc(pt_done, 1)

                def attend(pairs):
                    pe.wait_ge(qkv_out, pairs * 3)
                    v = qkv[:, 2]
                    for hh in range(2):
                        pe.wait_ge((pt_act, pt_dve)[hh], pairs)
                        hs = slice(hh * HD, hh * HD + HD)
                        T.matmul(ps[:, MISC, hh * S:(hh + 1) * S], v[:, 0, hs], pt[:, hh, 0:S],
                                 start=True, stop=False, skip_group_check=True)
                        last = T.matmul(ps[:, MISC, hh * S + P:(hh + 1) * S], v[:, 1, hs], pt[:, hh, S:S + P],
                                        start=False, stop=True, skip_group_check=True)
                    last.then_inc(pv_done, 1)

                def head_squares(pairs, bank):
                    pe.wait_ge(head_sq, pairs)
                    T.matmul(ps[:, bank], ones[:], silu_g[:].rearrange("p a b -> p (a b)"), start=True, stop=True)\
                        .then_inc(head_sum, 1)

                def scores(need):
                    pe.wait_ge(qkv_out, need)
                    q, k = qkv[:, 0], qkv[:, 1]
                    for hh in range(2):
                        for cc in range(units):
                            if l == 0:
                                rs = slice(0, P)
                                late, early = ps[:, 4, hh * S:(hh + 1) * S], ps[:, 5, hh * P:(hh + 1) * P]
                            else:
                                rs = slice(cc * HALF, (cc + 1) * HALF)
                                late = ps[:, 4 + cc, hh * S:(hh + 1) * S]
                                early = ps[:, (6, MISC)[cc], hh * P:(hh + 1) * P]
                            T.matmul(late, q[rs, hh, P:S], k[rs, hh, :], start=True, stop=True)
                            last = T.matmul(early, q[rs, hh, 0:P], k[rs, hh, 0:P], start=True, stop=True)
                    last.then_inc(s_done, 1)

                def pair(j, n, first):
                    pairs = j + PAIRS * l
                    col_slab(n, 8 * 2 * l if first else None)
                    col_slab(n + 1)
                    if not first:
                        turn_probs(pairs)
                        attend(pairs)
                    elif l == 0:
                        pe.wait_ge(bias_ready, 6)
                    v_slab(n + 2)
                    if l and not first:
                        head_squares(j, 7)
                    scores(pairs * 3 + 2)

                pair(0, Slab(ATTN[l]), True)
                with pe.Fori(1, PAIRS) as j:
                    pair(j, Slab(ATTN[l], 3, j), False)
                pairs = PAIRS * (l + 1)
                pe.wait_ge(o_ready, pairs - 1)
                pe.wait_ge(qkv_out, pairs * 3)
                for j in range(KT // 2):
                    if j == 2:
                        turn_probs(pairs)
                        attend(pairs)
                        if l == 0:
                            pe.wait_ge(ada_acc, 2 * 20)
                            reduce_mods(5, 3)
                        else:
                            pe.wait_ge(ada_acc, 2 * 48)
                            reduce_mods(5, 1)
                            head_squares(4, 4)
                    if j == 3:
                        pe.wait_ge(o_ready, pairs)
                    js = slice(2 * j, 2 * j + 2)
                    row_slab(Slab(OPROJ[l] + j), OP_ACC, o_hi[:, js], o_lo[:, js], j == 0, j == 3)
                sum_squares(1 + 4 * l)
                pe.wait_ge(y_copied, 4 * (2 * l + 1))
                clear_acc(FF_ACC)
                sum_squares(2 + 4 * l)

                def down(n, chunks, final):
                    pe.wait_ge(hid_lo_ready, chunks)
                    row_slab(n, FF_ACC, hid_hi[:], hid_lo[:], False, final)

                col_slab(Slab(FFN[l]), 8 * (2 * l + 1))
                col_slab(Slab(FFN[l] + 1))
                if l == 0:
                    pe.wait_ge(ada_acc, 2 * 24)
                    reduce_mods(MISC, 1)
                with pe.Fori(0, (FF_CHUNKS - 1) // 2) as i:
                    for c2 in range(2):
                        n = Slab(FFN[l] + 2 + 3 * c2, 6, i)
                        pe.wait_ge(hid_ready, i * 2 + (FF_CHUNKS * l + c2 + 1))
                        col_slab(n)
                        col_slab(n + 1)
                        if l == 0 and c2 == 1:
                            pe.wait_ge(ada_acc, i * 8 + 2 * 28)
                            pe.wait_ge(mod_ready, i + 6)
                            reduce_mods(MISC, 1)
                        down(n + 2, i * 2 + (FF_CHUNKS * l + c2 + 1), False)
                down(Slab(FFN[l] + 3 * FF_CHUNKS - 1), FF_CHUNKS * (l + 1), True)
                sum_squares(3 + 4 * l)
                sum_squares(4 + 4 * l)

            hb = 8 * 4
            for s in range(4):
                if s == 3:
                    pe.wait_ge(mix_out, 1)
                col_slab(Slab(MIX_IN + s), hb if s == 0 else None)
            pe.wait_ge(conv_done, 1)
            pe.wait_ge(late_loaded, 16 * N_LATE)
            pe.wait_ge(y_copied, 16)
            for g in range(2):
                for t in range(CT):
                    last = T.matmul(ps[:, 4 + 2 * g + t // 2, (t % 2) * S:(t % 2) * S + S], small_w[:, g, t],
                                    xb[:, t], start=True, stop=True)
                last.then_inc(gates_done, 1)
            pe.wait_ge(mix_out, 3)
            col_slab(Slab(MIX_IN + 4))
            col_slab(Slab(MIX_IN + 5))
            pe.wait_ge(pool_done, 1)
            pe.wait_ge(gates_out, 2)
            for t in range(CT):
                last = T.matmul(ps[:, 4 + t // 2, (t % 2) * S:(t % 2) * S + S], small_w[:, 2, t], pool_d[:, t],
                                start=True, stop=True)
            last.then_inc(pool_mm, 1)
            pe.wait_ge(gates_out, 4)
            pe.wait_ge(mix_out, 6)
            for j in range(KT // 2):
                pe.wait_ge(mix_ready, j // 2 + 1)
                js = slice(2 * j, 2 * j + 2)
                row_slab(Slab(MIX_OUT + j), OP_ACC, o_hi[:, js], o_lo[:, js], j == 0, j == 3)
            pe.wait_ge(x_ready, 4 * 6)
            clear_acc(FF_ACC)
            sum_squares(9)

            H0 = DEPTH * FF_CHUNKS
            col_slab(Slab(MLP), 8 * 5)
            with pe.Fori(0, (UP_CHUNKS - 1) // 3) as i:
                for c3 in range(3):
                    n = Slab(MLP + 1 + 2 * c3, 6, i)
                    pe.wait_ge(relu_ready, i * 3 + (c3 + 1))
                    col_slab(n)
                    pe.wait_ge(hid_lo_ready, i * 3 + (H0 + c3 + 1))
                    row_slab(n + 1, FF_ACC, hid_hi[:], hid_lo[:], False, False)
            for o in range(2):
                for t in range(ST):
                    last = T.transpose(ps[:, MISC, o * S + t * P:o * S + (t + 1) * P], p_in[:, t, o * P:(o + 1) * P],
                                       ident[:])
            last.then_inc(p_turned, 1)
            pe.wait_ge(hid_lo_ready, H0 + UP_CHUNKS)
            row_slab(Slab(MLP + 2 * UP_CHUNKS - 1), FF_ACC, hid_hi[:], hid_lo[:], False, True)
            pe.wait_ge(x_ready, 4 * 6 + 1)
            pe.wait_ge(p_lo_ready, 1)
            row_slab(Slab(PLE_PROJ), [0, 1, 2, 4], hid_hi[:], hid_lo[:], True, True)
            sum_squares(10)
            pe.wait_ge(proj_out, 4)
            for j in range(4):
                if j == 3:
                    pe.wait_ge(gate_out, 1)
                col_slab(Slab(PLE_GATE + j), 8 * 6 if j == 0 else None)
            sum_squares(11)
            for half in range(2):
                pe.wait_ge(final_ready, 4 * half + 4)
                for t in range(ST):
                    for f in range(4):
                        last = T.transpose(ps[:, 4 + 2 * t + half, f * P:(f + 1) * P],
                                           y[:, 4 * half + f, t * P:(t + 1) * P], ident[:])
                    last.then_inc(final_turned, 1)

        @block.scalar
        def _(act):
            def split_hi(n):
                if n.first >= N_SLABS:
                    return
                act.wait_ge(slab_loaded[n.place], n.turn * 16 + 16)
                if n.stride or n.first >= RING:
                    act.wait_ge(slab_done, n.plus(1 - RING))
                A.activation(w_hi[:, n.place], raw[:, n.place], ACT.Copy).then_inc(slab_hi, 1)

            def norm(k, src, wait):
                A.preload_act_table(ACT.Sqrt)
                for b in range(KT // 2):
                    wait(b)
                    if 4 * k + b >= 2:
                        act.wait_ge(sq_used, 4 * k + b - 1)
                    A.activation(sq[:, b % 2], src[:, 2 * b:2 * b + 2], ACT.Square).then_inc(sq_ready, 1)
                act.wait_ge(sq_used, 4 * k + 4)
                A.activation(rms[:], ps[:, MISC, 0:S], ACT.Sqrt, bias=eps[:, 0:1], scale=1.0 / D)\
                    .then_inc(rms_ready, 1)

            def norm_x(k, update):
                norm(k, xt, lambda b: act.wait_ge(x_ready, 4 * update + b + 1))

            def norm_y(k, i):
                norm(k, y, lambda b: act.wait_ge(y_copied, 4 * i + b + 1))

            def h_high(i, shift):
                for t in range(KT):
                    act.wait_ge(h_norm, 8 * i + t + 1)
                    if shift is None:
                        A.activation(h_hi[:, t], y[:, t], ACT.Copy).then_inc(h_hi_ready, 1)
                    else:
                        A.activation(h_hi[:, t], y[:, t], ACT.Identity, bias=mods[:, shift, t:t + 1])\
                            .then_inc(h_hi_ready, 1)

            act.wait_ge(tab_ready, 1)
            A.activation(c_act[:], tabA[:, ROW_C:ROW_C + KT], ACT.Silu).then_inc(c_ready, 1)
            for b in range(4):
                act.wait_ge(x_turned, b + 1)
                A.activation(xt[:, 2 * b:2 * b + 2], ps[:, 4 + b], ACT.Copy).then_inc(x_ready, 1)
            act.wait_ge(const_ready, 3)
            norm_x(0, 0)
            split_hi(Slab(0))
            split_hi(Slab(1))
            h_high(0, SH_A)
            for b, bank in enumerate(FLIP_BANKS):
                act.wait_ge(bias_turned, b + 1)
                A.activation(bias_flat[:, b * 512:(b + 1) * 512], ps[:, bank], ACT.Copy).then_inc(bias_ready, 1)

            for l in range(DEPTH):
                units = 1 + l

                def exps(pairs):
                    act.wait_ge(s_negmax, pairs)
                    for u in range(2 * units):
                        A.activation(prob[:, u, 0:S], prob[:, u, 0:S], ACT.Exp, bias=maxes[:, 0, u:u + 1],
                                     accum_out=sums[:, 0, u:u + 1])
                        last = A.activation(prob[:, u, S:S + P], prob[:, u, S:S + P], ACT.Exp,
                                            bias=maxes[:, 1, u:u + 1], accum_out=sums[:, 1, u:u + 1])
                    last.then_inc(s_exp, 1)

                def copy_turned(pairs):
                    act.wait_ge(pt_done, pairs * 2 - 1)
                    A.activation(pt[:, 0], ps[:, 5, 0:LINE], ACT.Copy).then_inc(pt_act, 1)

                def heads_out(pairs, at):
                    act.wait_ge(pv_done, pairs)
                    if l == 0:
                        A.activation(o_hi[:, at], ps[:, MISC], ACT.Copy).then_inc(o_hi_ready, 1)
                    else:
                        A.activation(hid[:], ps[:, MISC], ACT.Copy).then_inc(head_copied, 1)
                        A.activation(silu_g[:], ps[:, MISC], ACT.Square).then_inc(head_sq, 1)

                def heads_norm(j, at, bank):
                    act.wait_ge(head_sum, j)
                    A.activation(sq[:, 0], ps[:, bank], ACT.Sqrt, bias=eps[:, 0:1], scale=1.0 / HD)\
                        .then_inc(head_rms, 1)
                    act.wait_ge(head_norm, j)
                    A.activation(o_hi[:, at], hid[:], ACT.Copy).then_inc(o_hi_ready, 1)

                def pair(j, n, first):
                    pairs = j + PAIRS * l
                    if not first:
                        exps(pairs)
                    split_hi(n + 2)
                    act.wait_ge(slab_done, n.plus(1))
                    A.activation(qkv[:, 0], ps[:, n.place], ACT.Copy, scale=(HALF if l else HD) ** -0.5)\
                        .then_inc(qkv_out, 1)
                    split_hi(n + 3)
                    if not first:
                        copy_turned(pairs)
                    act.wait_ge(slab_done, n.plus(2))
                    A.activation(qkv[:, 1], ps[:, (n + 1).place], ACT.Copy).then_inc(qkv_out, 1)
                    split_hi(n + 4)
                    if not first:
                        heads_out(pairs, ds(2 * j - 2, 2))
                    act.wait_ge(slab_done, n.plus(3))
                    A.activation(qkv[:, 2], ps[:, (n + 2).place], ACT.Copy).then_inc(qkv_out, 1)
                    if l and not first:
                        heads_norm(j, ds(2 * j - 2, 2), 7)

                pair(0, Slab(ATTN[l]), True)
                with act.Fori(1, PAIRS) as j:
                    pair(j, Slab(ATTN[l], 3, j), False)
                pairs = PAIRS * (l + 1)
                n = Slab(OPROJ[l])
                exps(pairs)
                split_hi(n + 2)
                split_hi(n + 3)
                copy_turned(pairs)
                heads_out(pairs, slice(6, 8))
                if l:
                    heads_norm(4, slice(6, 8), 4)
                split_hi(n + 4)
                split_hi(n + 5)
                norm_y(1 + 4 * l, 2 * l)
                norm_x(2 + 4 * l, 2 * l + 1)
                h_high(2 * l + 1, 6 * l + SH_F)

                def gated(n, chunk):
                    act.wait_ge(slab_done, n.plus(1))
                    A.activation(silu_g[:], ps[:, n.place], ACT.Silu).then_inc(silu_ready, 1)

                def hidden_hi(chunk):
                    act.wait_ge(hid_ready, chunk)
                    A.activation(hid_hi[:], hid[:], ACT.Copy).then_inc(hid_hi_ready, 1)

                A.preload_act_table(ACT.Silu)
                n = Slab(FFN[l])
                split_hi(n + 2)
                gated(n, 0)
                split_hi(n + 3)
                hidden_hi(FF_CHUNKS * l + 1)
                with act.Fori(0, (FF_CHUNKS - 1) // 2) as i:
                    for c2 in range(2):
                        n = Slab(FFN[l] + 2 + 3 * c2, 6, i)
                        split_hi(n + 2)
                        gated(n, 0)
                        split_hi(n + 3)
                        split_hi(n + 4)
                        act.wait_ge(slab_done, n.plus(3))
                        hidden_hi(i * 2 + (FF_CHUNKS * l + c2 + 2))
                split_hi(Slab(FFN[l] + 3 * FF_CHUNKS + 1))
                norm_y(3 + 4 * l, 2 * l + 1)
                norm_x(4 + 4 * l, 2 * l + 2)
                h_high(2 * l + 2, 6 * (l + 1) + SH_A if l == 0 else None)
                if l == 0:
                    act.wait_ge(lam_step, 2)
                    A.activation(lam_s[:, 2:4], lam_s[:, 0:2], ACT.Exp).then_inc(lam_exp, 1)
                    act.wait_ge(lruc_step, 2)
                    A.activation(lruc[:, 2], lruc[:, 1], ACT.Exp).then_inc(lruc_exp, 1)

            n = Slab(MIX_IN)

            def branch(s, dst, func):
                act.wait_ge(slab_done, MIX_IN + s + 1)
                A.activation(dst, ps[:, (MIX_IN + s) % RING], func).then_inc(mix_out, 1)

            split_hi(n + 2)
            act.wait_ge(pads_zero, 2)
            branch(0, ul[:, 0:2, PADC:PADC + S], ACT.Copy)
            split_hi(n + 3)
            branch(1, ul[:, 2:4, PADC:PADC + S], ACT.Copy)
            split_hi(n + 4)
            branch(2, up[:, 0:2, PADW:PADW + S], ACT.Copy)
            split_hi(n + 5)
            branch(3, up[:, 2:4, PADW:PADW + S], ACT.Copy)
            split_hi(n + 6)
            for g, dst in enumerate((gate_r, gate_i)):
                act.wait_ge(gates_done, g + 1)
                for t in range(CT):
                    b = tabB[:, R_GA_B + t:R_GA_B + t + 1] if g == 0 else tabC[:, R_GX_B + t:R_GX_B + t + 1]
                    last = A.activation(dst[:, t], ps[:, 4 + 2 * g + t // 2, (t % 2) * S:(t % 2) * S + S],
                                        ACT.Sigmoid, bias=b)
                    if t % 2 == 1:
                        last.then_inc(gates_out, 1)
            act.wait_ge(gates_out, 2)
            act.wait_ge(lruc_step, LRUC_STEPS)
            for t in range(CT):
                A.activation(a_t[:, t], gate_r[:, t], ACT.Exp, scale=lruc[:, 7, t:t + 1])
                last = A.activation(th[:, t], gate_r[:, t], ACT.Tanh, scale=lruc[:, 7, t:t + 1])
            last.then_inc(lru_exp, 1)
            act.wait_ge(lru_step, 2)
            A.activation(mult[:], th[:], ACT.Sqrt, scale=-1.0).then_inc(lru_mult, 1)
            branch(4, gelu_t[:, 0:2], ACT.Gelu_apprx_tanh)
            split_hi(n + 7)
            branch(5, gelu_t[:, 2:4], ACT.Gelu_apprx_tanh)
            split_hi(n + 8)
            act.wait_ge(pool_out, 1)
            A.activation(o_hi[:, 0:CT], pool_d[:], ACT.Copy).then_inc(mix_hi, 1)
            split_hi(n + 9)
            act.wait_ge(lru_ready, 1)
            A.activation(o_hi[:, CT:2 * CT], lru_h[:], ACT.Copy).then_inc(mix_hi, 1)
            split_hi(n + 10)
            split_hi(n + 11)
            norm_x(9, 5)
            h_high(5, None)

            H0 = DEPTH * FF_CHUNKS

            def rectified(n):
                act.wait_ge(slab_done, n.plus(1))
                A.activation(silu_g[:], ps[:, n.place], ACT.Relu).then_inc(relu_ready, 1)

            n = Slab(MLP)
            split_hi(n + 2)
            rectified(n)
            act.wait_ge(hid_ready, H0 + 1)
            A.activation(hid_hi[:], hid[:], ACT.Copy).then_inc(hid_hi_ready, 1)
            with act.Fori(0, (UP_CHUNKS - 1) // 3) as i:
                for c3 in range(3):
                    n = Slab(MLP + 1 + 2 * c3, 6, i)
                    split_hi(n + 2)
                    rectified(n)
                    split_hi(n + 3)
                    act.wait_ge(slab_done, n.plus(2))
                    act.wait_ge(hid_ready, i * 3 + (H0 + c3 + 2))
                    A.activation(hid_hi[:], hid[:], ACT.Copy).then_inc(hid_hi_ready, 1)
            split_hi(Slab(MLP + 2 * UP_CHUNKS + 1))
            act.wait_ge(p_turned, 1)
            act.wait_ge(slab_done, MLP + 2 * UP_CHUNKS)
            A.activation(hid_hi[:], ps[:, MISC], ACT.Copy).then_inc(p_hi_ready, 1)
            norm_banks = [0, 1, 2, 4]
            norm_x(10, 6)
            for b in range(4):
                if b < 3:
                    act.wait_ge(acc_done, 3 * 6 + b + 1)
                else:
                    act.wait_ge(slab_done, PLE_PROJ + 1)
                A.activation(proj[:, 2 * b:2 * b + 2], ps[:, norm_banks[b]], ACT.Copy).then_inc(proj_out, 1)
            split_hi(Slab(PLE_PROJ + 2))
            h_high(6, None)
            split_hi(Slab(PLE_GATE + 2))
            for j in range(4):
                if j:
                    act.wait_ge(gate_mixed, j)
                act.wait_ge(slab_done, PLE_GATE + j + 1)
                for o in range(2):
                    t = 2 * j + o
                    last = A.activation(gate[:, o], ps[:, (PLE_GATE + j) % RING, o * S:(o + 1) * S], ACT.Sigmoid,
                                        bias=tabB[:, R_PLE_B + t:R_PLE_B + t + 1])
                last.then_inc(gate_out, 1)
                split_hi(Slab(PLE_GATE + j + 3))
            norm_x(11, 7)
            for t in range(ST):
                act.wait_ge(final_turned, t + 1)
                A.activation(out_tok[:, t, 0:512], ps[:, 4 + 2 * t], ACT.Copy).then_inc(out_act, 1)

        @block.vector
        def _(dve):
            def split_lo(n):
                if n.first >= N_SLABS:
                    return
                dve.wait_ge(slab_hi, n.plus(1))
                V.tensor_tensor(w_lo[:, n.place], raw[:, n.place], w_hi[:, n.place].bitcast(F32),
                                ALU.subtract).then_inc(slab_lo, 1)

            def ada(m, place, count, slot, scalars, fresh):
                dve.wait_ge(ada_loaded[place], count)
                for k in range(2):
                    if fresh and k == 0:
                        V.tensor_scalar(ada_sum[:, slot], ada_raw[:, place, k], scalars[k], None, ALU.mult)\
                            .then_inc(ada_acc, 1)
                    else:
                        dve.wait_ge(ada_acc, m * 2 + k)
                        V.scalar_tensor_tensor(out=ada_sum[:, slot], in0=ada_raw[:, place, k], scalar=scalars[k],
                                               in1=ada_sum[:, slot], op0=ALU.mult, op1=ALU.add)\
                            .then_inc(ada_acc, 1)

            def c_cols(kp):
                return [c_act[:, 2 * kp + k:2 * kp + k + 1] for k in range(2)]

            def ada_static(m, slot):
                ada(m, (m + 1) % 3, 16 * ((m + 1) // 3 + (0 if (m + 1) % 3 == 0 else 1)), slot, c_cols(m % 4),
                    m % 4 == 0)

            def mod(g, bank, s):
                V.tensor_tensor(mods[:, g], ps[:, bank, s * KT:(s + 1) * KT], tabA[:, g * KT:(g + 1) * KT], ALU.add)\
                    .then_inc(mod_ready, 1)

            def gain_of(i):
                l, k = i // 4, i % 4
                g = 6 * l + (SC_A, G_A, SC_F, G_F)[k]
                dve.wait_ge(mod_ready, g + 1)
                V.scalar_tensor_tensor(out=gain[:, i], in0=mods[:, g], scalar=1.0 if k % 2 == 0 else 0.0,
                                       in1=tabB[:, R_NORM + i * KT:R_NORM + (i + 1) * KT], op0=ALU.add,
                                       op1=ALU.mult).then_inc(gain_ready, 1)

            def inverse_rms(k):
                dve.wait_ge(rms_ready, k + 1)
                V.reciprocal(rstd[:], rms[:]).then_inc(rstd_ready, 1)
                dve.wait_ge(rstd_ready, k + 1)

            def h_input(k, i, gains, shift):
                inverse_rms(k)

                def low(t):
                    dve.wait_ge(h_hi_ready, 8 * i + t + 1)
                    if shift is None:
                        V.tensor_tensor(h_lo[:, t], y[:, t], h_hi[:, t].bitcast(F32), ALU.subtract)\
                            .then_inc(h_ready, 1)
                    else:
                        V.scalar_tensor_tensor(out=h_lo[:, t], in0=y[:, t], scalar=mods[:, shift, t:t + 1],
                                               in1=h_hi[:, t].bitcast(F32), op0=ALU.add, op1=ALU.subtract)\
                            .then_inc(h_ready, 1)

                for t in range(KT):
                    V.scalar_tensor_tensor(out=y[:, t], in0=xt[:, t], scalar=gains[:, t:t + 1], in1=rstd[:],
                                           op0=ALU.mult, op1=ALU.mult).then_inc(h_norm, 1)
                    if t:
                        low(t - 1)
                low(KT - 1)

            def bank_done(b, sums, slab):
                if b < 3:
                    dve.wait_ge(acc_done, 3 * sums + b + 1)
                else:
                    dve.wait_ge(slab_done, slab + 1)

            def add_y(k, i, banks, slab, gains):
                for b in range(4):
                    bank_done(b, i, slab)
                    V.tensor_copy(y[:, 2 * b:2 * b + 2], ps[:, banks[b]]).then_inc(y_copied, 1)
                inverse_rms(k)
                for t in range(KT):
                    V.scalar_tensor_tensor(out=y[:, t], in0=y[:, t], scalar=gains[:, t:t + 1], in1=rstd[:],
                                           op0=ALU.mult, op1=ALU.mult).then_inc(y_scaled, 1)
                    if t % 2 and t > 1:
                        add_pair(i, t // 2 - 1)
                add_pair(i, 3)

            def add_pair(i, b):
                dve.wait_ge(y_scaled, 8 * i + 2 * b + 2)
                V.tensor_tensor(xt[:, 2 * b:2 * b + 2], xt[:, 2 * b:2 * b + 2], y[:, 2 * b:2 * b + 2], ALU.add)\
                    .then_inc(x_ready, 1)

            def add_acc(sums, banks, slab):
                for b in range(4):
                    bank_done(b, sums, slab)
                    V.tensor_tensor(xt[:, 2 * b:2 * b + 2], xt[:, 2 * b:2 * b + 2],
                                    ps[:, banks[b]].rearrange("p (o s) -> p o s", o=2), ALU.add)\
                        .then_inc(x_ready, 1)

            V.memset(ones[:], 1.0).then_inc(const_ready, 1)
            V.memset(zeros[:], 0.0).then_inc(const_ready, 1)
            V.memset(eps[:], EPS).then_inc(const_ready, 1)
            dve.wait_ge(tab_turned, 1)
            V.tensor_copy(tabA[:, 0:ROW_C + KT], ps[:, 0, 0:ROW_C + KT]).then_inc(tab_ready, 1)
            dve.wait_ge(rel_turned, 1)
            V.tensor_copy(rel_t[:], ps[0:HEADS, 1, 0:N_BUCKETS]).then_inc(rel_ready, 1)
            dve.wait_ge(c_ready, 1)
            for m in range(8):
                if m == 4:
                    dve.wait_ge(tab_turned, 2)
                    V.tensor_copy(tabB[:], ps[:, 2, 0:P]).then_inc(tab_ready, 1)
                    dve.wait_ge(tab_turned, 3)
                    V.tensor_copy(tabC[:, 0:R_SUBLN + 1], ps[:, 0, 0:R_SUBLN + 1]).then_inc(tab_ready, 1)
                ada_static(m, m // 4)
            split_lo(Slab(0))
            dve.wait_ge(ada_reduced, 1)
            dve.wait_ge(tab_ready, 3)
            mod(0, 1, 0)
            mod(1, 1, 1)
            gain_of(0)
            dve.wait_ge(gain_ready, 1)
            h_input(0, 0, gain[:, 0], SH_A)
            split_lo(Slab(1))

            for l in range(DEPTH):
                units = 1 + l

                def biased(pairs, h0):
                    dve.wait_ge(s_done, pairs)
                    if l == 0:
                        V.tensor_tensor(prob[:, 0:2, 0:S], ps[:, 4].rearrange("p (h s) -> p h s", h=2),
                                        bias[:, ds(h0, 2), 0:S], ALU.add)
                        last = V.tensor_tensor(prob[:, 0:2, S:S + P], ps[:, 5, 0:S].rearrange("p (h s) -> p h s", h=2),
                                               bias[:, ds(h0, 2), S:S + P], ALU.add)
                    else:
                        for hh in range(2):
                            for cc in range(2):
                                V.tensor_tensor(prob[:, 2 * hh + cc:2 * hh + cc + 1, 0:S],
                                                ps[:, 4 + cc:5 + cc, hh * S:(hh + 1) * S],
                                                bias[:, ds(h0 + hh, 1), 0:S], ALU.add)
                                u, b = 2 * hh + cc, (6, MISC)[cc]
                                last = V.tensor_tensor(prob[:, u:u + 1, S:S + P], ps[:, b:b + 1, hh * P:(hh + 1) * P],
                                                       bias[:, ds(h0 + hh, 1), S:S + P], ALU.add)
                    last.then_inc(s_biased, 1)
                    dve.wait_ge(s_biased, pairs)
                    U = 2 * units
                    V.tensor_reduce(sums[:, 0, 0:U], prob[:, 0:U, 0:S], AX_X, ALU.max)
                    V.tensor_reduce(sums[:, 1, 0:U], prob[:, 0:U, S:S + P], AX_X, ALU.max).then_inc(s_max, 1)
                    dve.wait_ge(s_max, pairs)
                    V.tensor_scalar(maxes[:, :, 0:U], sums[:, :, 0:U], -1.0, None, ALU.mult).then_inc(s_negmax, 1)

                def normalised(pairs, j):
                    U = 2 * units
                    dve.wait_ge(s_exp, pairs)
                    V.reciprocal(rsums[:, :, 0:U], sums[:, :, 0:U]).then_inc(s_rsum, 1)
                    dve.wait_ge(s_rsum, pairs)
                    if l == 0:
                        for u in range(2):
                            for part, at in ((0, slice(0, S)), (1, slice(S, S + P))):
                                last = V.tensor_scalar(prob[:, u, at], prob[:, u, at], rsums[:, part, u:u + 1],
                                                       None, ALU.mult)
                        last.then_inc(p_ready, 1)
                        return
                    V.tensor_scalar(rsums[:, :, 1:4:2], rsums[:, :, 1:4:2], neg_lam[:, 0:1], None, ALU.mult)\
                        .then_inc(s_mixed, 1)
                    dve.wait_ge(s_mixed, j * 2 - 1)
                    for hh in range(2):
                        for part, at in ((0, slice(0, S)), (1, slice(S, S + P))):
                            u = 2 * hh + 1
                            last = V.tensor_scalar(prob[:, u, at], prob[:, u, at], rsums[:, part, u:u + 1],
                                                   None, ALU.mult)
                    last.then_inc(s_mixed, 1)
                    dve.wait_ge(s_mixed, j * 2)
                    for hh in range(2):
                        for part, at in ((0, slice(0, S)), (1, slice(S, S + P))):
                            u = 2 * hh
                            last = V.scalar_tensor_tensor(out=prob[:, u, at], in0=prob[:, u, at],
                                                          scalar=rsums[:, part, u:u + 1], in1=prob[:, u + 1, at],
                                                          op0=ALU.mult, op1=ALU.add)
                    last.then_inc(p_ready, 1)

                def copy_turned(pairs):
                    dve.wait_ge(pt_done, pairs * 2)
                    V.tensor_copy(pt[:, 1], ps[:, 6, 0:LINE]).then_inc(pt_dve, 1)

                def heads_low(pairs, j, at):
                    if l == 0:
                        dve.wait_ge(o_hi_ready, pairs)
                        V.tensor_tensor(o_lo[:, at], ps[:, MISC].rearrange("p (h s) -> p h s", h=2),
                                        o_hi[:, at].bitcast(F32), ALU.subtract).then_inc(o_ready, 1)
                        return
                    dve.wait_ge(head_rms, j)
                    V.reciprocal(sq[:, 1], sq[:, 0]).then_inc(head_rstd, 1)
                    dve.wait_ge(head_rstd, j)
                    V.scalar_tensor_tensor(out=hid[:], in0=hid[:], scalar=subln[:, 0:1], in1=sq[:, 1],
                                           op0=ALU.mult, op1=ALU.mult).then_inc(head_norm, 1)
                    dve.wait_ge(o_hi_ready, pairs)
                    V.tensor_tensor(o_lo[:, at], hid[:], o_hi[:, at].bitcast(F32), ALU.subtract).then_inc(o_ready, 1)

                def pair(j, n, first):
                    pairs = j + PAIRS * l
                    if not first:
                        biased(pairs, 2 * j - 2)
                    split_lo(n + 2)
                    V.tensor_copy(c_pair[:], c_act[:, ds(2 * j, 2)]).then_inc(c_pair_ready, 1)
                    dve.wait_ge(c_pair_ready, pairs + 1)
                    cs = [c_pair[:, k:k + 1] for k in range(2)]

                    def step_ada(c3):
                        if l == 0:
                            ada(j * 3 + (8 + c3), c3, j * 16 + 16 * (3 + (c3 > 0)), c3, cs, first)
                        elif c3 == 0:
                            ada(j + 44, 2, j * 16 + 16 * 9, 0, cs, first)
                    step_ada(0)
                    if not first:
                        normalised(pairs, j)
                    split_lo(n + 3)
                    step_ada(1)
                    if not first:
                        copy_turned(pairs)
                    split_lo(n + 4)
                    step_ada(2)
                    if not first:
                        heads_low(pairs, j, ds(2 * j - 2, 2))

                if l == 0:
                    dve.wait_ge(bias_ready, 6)
                pair(0, Slab(ATTN[l]), True)
                with dve.Fori(1, PAIRS) as j:
                    pair(j, Slab(ATTN[l], 3, j), False)
                pairs = PAIRS * (l + 1)
                n = Slab(OPROJ[l])
                biased(pairs, 2 * PAIRS - 2)
                split_lo(n + 2)
                normalised(pairs, 4)
                split_lo(n + 3)
                copy_turned(pairs)
                heads_low(pairs, 4, slice(6, 8))
                split_lo(n + 4)
                dve.wait_ge(ada_reduced, 2 if l == 0 else 9)
                if l == 0:
                    for s in range(3):
                        mod(G_A + s, 5, s)
                    gain_of(1)
                    gain_of(2)
                    ada_static(20, 0)
                    ada_static(21, 0)
                else:
                    mod(11, 5, 0)
                    gain_of(7)
                split_lo(n + 5)
                dve.wait_ge(gain_ready, 3 if l == 0 else 8)
                add_y(1 + 4 * l, 2 * l, OP_ACC, OPROJ[l] + 3, gain[:, 4 * l + 1])
                h_input(2 + 4 * l, 2 * l + 1, gain[:, 4 * l + 2], 6 * l + SH_F)

                def hidden(n, chunk):
                    dve.wait_ge(silu_ready, chunk)
                    dve.wait_ge(slab_done, n.plus(2))
                    if not isinstance(chunk, int) or chunk > 1:
                        dve.wait_ge(hid_lo_ready, chunk - 1)
                    V.tensor_tensor(hid[:], silu_g[:], ps[:, (n + 1).place].rearrange("p (o s) -> p o s", o=2),
                                    ALU.mult).then_inc(hid_ready, 1)

                def hidden_lo(chunk):
                    dve.wait_ge(hid_hi_ready, chunk)
                    V.tensor_tensor(hid_lo[:], hid[:], hid_hi[:].bitcast(F32), ALU.subtract)\
                        .then_inc(hid_lo_ready, 1)

                n = Slab(FFN[l])
                split_lo(n + 2)
                if l == 0:
                    ada_static(22, 0)
                    ada_static(23, 0)
                split_lo(n + 3)
                hidden(n, FF_CHUNKS * l + 1)
                hidden_lo(FF_CHUNKS * l + 1)
                if l == 0:
                    dve.wait_ge(ada_reduced, 3)
                    mod(G_F, MISC, 0)
                    gain_of(3)
                with dve.Fori(0, (FF_CHUNKS - 1) // 2) as i:
                    for c2 in range(2):
                        n = Slab(FFN[l] + 2 + 3 * c2, 6, i)
                        chunk = i * 2 + (FF_CHUNKS * l + c2 + 2)

                        def step_ada(kp):
                            ada(i * 4 + (24 + kp), (kp + 1) % 2, i * 32 + 16 * (9 + kp // 2), 0, c_cols(kp), kp == 0)

                        split_lo(n + 2)
                        if l == 0:
                            step_ada(2 * c2) if c2 == 0 else step_ada(3)
                        split_lo(n + 3)
                        if l == 0 and c2 == 0:
                            step_ada(1)
                        hidden(n, chunk)
                        split_lo(n + 4)
                        if l == 0 and c2 == 0:
                            step_ada(2)
                        hidden_lo(chunk)
                        if l == 0 and c2 == 1:
                            dve.wait_ge(ada_reduced, i + 4)
                            V.tensor_tensor(mods[:, ds(i + 6, 1)], ps[:, MISC:MISC + 1, 0:KT],
                                            tabA[:, ds(i * KT + 6 * KT, KT)].rearrange("p (a b) -> p a b", a=1),
                                            ALU.add).then_inc(mod_ready, 1)
                split_lo(Slab(FFN[l] + 3 * FF_CHUNKS + 1))
                if l == 0:
                    for i in (4, 5, 6):
                        gain_of(i)
                    dve.wait_ge(lam_loaded, 16)
                    V.tensor_tensor(lam_prod[:], lam_in[:, 0:4:2], lam_in[:, 1:4:2], ALU.mult).then_inc(lam_step, 1)
                    V.tensor_scalar(lruc[:, 0], tabC[:, R_L:R_L + CT], -1.0, None, ALU.mult).then_inc(lruc_step, 1)
                    V.tensor_scalar(subln[:], tabC[:, R_SUBLN:R_SUBLN + 1], 1.0 - LAMBDA_INIT, None, ALU.mult)
                    dve.wait_ge(lam_step, 1)
                    V.tensor_reduce(lam_s[:, 0:2], lam_prod[:], AX_X, ALU.add).then_inc(lam_step, 1)
                    dve.wait_ge(lruc_step, 1)
                    V.tensor_tensor(lruc[:, 1], tabC[:, R_L:R_L + CT], lruc[:, 0], ALU.min).then_inc(lruc_step, 1)
                    dve.wait_ge(gain_ready, 7)
                add_y(3 + 4 * l, 2 * l + 1, FF_ACC, FFN[l] + 3 * FF_CHUNKS - 1, gain[:, 4 * l + 3])
                if l == 0:
                    h_input(4, 2, gain[:, 4], 6 + SH_A)
                    dve.wait_ge(lam_exp, 1)
                    V.tensor_tensor(lam_s[:, 0:1], lam_s[:, 3:4], lam_s[:, 2:3], ALU.subtract).then_inc(lam_step, 1)
                    dve.wait_ge(lam_step, 3)
                    V.tensor_scalar(neg_lam[:], lam_s[:, 0:1], -LAMBDA_INIT, None, ALU.add).then_inc(lam_step, 1)
                    dve.wait_ge(lam_step, 4)
                    dve.wait_ge(lruc_exp, 1)
                    done = [2]

                    def step(ins):
                        done[0] += 1
                        ins.then_inc(lruc_step, 1)
                        dve.wait_ge(lruc_step, done[0])

                    u, s1, s2, q = lruc[:, 2], lruc[:, 3], lruc[:, 4], lruc[:, 5]
                    step(V.tensor_scalar(s1, u, 2.0, None, ALU.add))
                    step(V.reciprocal(s1, s1))
                    step(V.tensor_tensor(s1, s1, u, ALU.mult))
                    step(V.tensor_tensor(s2, s1, s1, ALU.mult))
                    step(V.tensor_scalar(q, s2, 1.0 / 17, None, ALU.mult))
                    for m in range(7, 0, -1):
                        step(V.scalar_tensor_tensor(out=q, in0=q, scalar=1.0 / (2 * m + 1), in1=s2, op0=ALU.add,
                                                    op1=ALU.mult))
                    step(V.scalar_tensor_tensor(out=q, in0=q, scalar=1.0, in1=s1, op0=ALU.add, op1=ALU.mult))
                    step(V.tensor_scalar(lruc[:, 6], tabC[:, R_L:R_L + CT], 0.0, LRU_C, ALU.min, ALU.mult))
                    step(V.scalar_tensor_tensor(out=lruc[:, 7], in0=q, scalar=-2.0 * LRU_C, in1=lruc[:, 6],
                                                op0=ALU.mult, op1=ALU.add))
                    assert done[0] == LRUC_STEPS
                else:
                    h_input(8, 4, tabB[:, R_MIX:R_MIX + KT], None)

            n = Slab(MIX_IN)
            V.memset(ul[:, :, 0:PADC], 0.0).then_inc(pads_zero, 1)
            V.memset(up[:, :, 0:PADW], 0.0).then_inc(pads_zero, 1)
            V.memset(win[0][:, :, 0:PADW], 0.0)
            V.memset(win[1][:, :, 0:PADW], 0.0).then_inc(pads_zero, 1)
            split_lo(n + 2)
            split_lo(n + 3)

            def conv(t0, steps):
                for k in range(CONV):
                    for t in (t0, t0 + 1):
                        w = tabB[:, R_CONV_W + k * CT + t:R_CONV_W + k * CT + t + 1]
                        if k == 0:
                            last = V.tensor_scalar(xb[:, t], ul[:, t, 0:S], w, tabB[:, R_CONV_B + t:R_CONV_B + t + 1],
                                                   ALU.mult, ALU.add)
                        else:
                            last = V.scalar_tensor_tensor(out=xb[:, t], in0=ul[:, t, k:k + S], scalar=w,
                                                          in1=xb[:, t], op0=ALU.mult, op1=ALU.add)
                        last.then_inc(conv_step, 1)
                    if k < CONV - 1:
                        dve.wait_ge(conv_step, steps + 2 * k + 2)

            dve.wait_ge(mix_out, 1)
            conv(0, 0)
            dve.wait_ge(mix_out, 2)
            split_lo(n + 4)
            conv(2, 2 * CONV)
            dve.wait_ge(conv_step, 4 * CONV)
            V.memset(lruc[:, 0], 0.0).then_inc(conv_done, 1)
            split_lo(n + 5)
            dve.wait_ge(mix_out, 3)
            dve.wait_ge(pads_zero, 3)
            dve.wait_ge(mix_out, 4)
            src = up
            for g in range(len(POOL_WINDOWS)):
                dst, lag = win[g % 2], 1 << g
                V.tensor_tensor(dst[:, g:CT, PADW:], src[:, g:CT, PADW:], src[:, g:CT, PADW - lag:PADW - lag + S],
                                ALU.add).then_inc(pool_step, 1)
                dve.wait_ge(pool_step, g + 1)
                src = dst
            split_lo(n + 6)
            dve.wait_ge(inv_ready, 1)
            for g, w in enumerate(POOL_WINDOWS):
                V.scalar_tensor_tensor(out=pool_d[:, g, w:S], in0=win[g % 2][:, g, PADW + w:], scalar=1.0 / w,
                                       in1=up[:, g, PADW + w:], op0=ALU.mult, op1=ALU.subtract)
            for g, w in enumerate(POOL_WINDOWS):
                last = V.tensor_tensor(pool_d[:, g, 0:w], win[g % 2][:, g, PADW:PADW + w], inv_t[:, 0:w], ALU.mult)
            last.then_inc(pool_step, 1)
            dve.wait_ge(pool_step, 5)
            for g, w in enumerate(POOL_WINDOWS):
                last = V.tensor_tensor(pool_d[:, g, 0:w], pool_d[:, g, 0:w], up[:, g, PADW:PADW + w], ALU.subtract)
            last.then_inc(pool_done, 1)
            dve.wait_ge(gates_out, 4)
            V.tensor_tensor(gate_i[:], gate_i[:], xb[:], ALU.mult).then_inc(lru_in, 1)
            dve.wait_ge(lru_exp, 1)
            V.tensor_tensor(mult[:], a_t[:], a_t[:], ALU.mult).then_inc(lru_step, 1)
            dve.wait_ge(lru_step, 1)
            V.scalar_tensor_tensor(out=th[:], in0=mult[:], scalar=1.0, in1=th[:], op0=ALU.add, op1=ALU.mult)\
                .then_inc(lru_step, 1)
            split_lo(n + 7)
            dve.wait_ge(lru_mult, 1)
            V.memset(mult[:, :, 0:1], 1.0).then_inc(lru_in, 1)
            dve.wait_ge(lru_in, 2)
            V.tensor_tensor(gate_i[:], gate_i[:], mult[:], ALU.mult).then_inc(lru_in, 1)
            dve.wait_ge(pool_mm, 1)
            for t in range(CT):
                last = V.tensor_scalar(pool_d[:, t], ps[:, 4 + t // 2, (t % 2) * S:(t % 2) * S + S],
                                       tabC[:, R_POOL_B + t:R_POOL_B + t + 1], tabC[:, R_POOL_S + t:R_POOL_S + t + 1],
                                       ALU.add, ALU.mult)
            last.then_inc(pool_out, 1)
            dve.wait_ge(lru_in, 3)
            for t in range(CT):
                last = V.tensor_tensor_scan(lru_h[:, t], a_t[:, t], gate_i[:, t], 0.0, ALU.mult, ALU.add)
            last.then_inc(lru_scan, 1)
            split_lo(n + 8)
            dve.wait_ge(mix_hi, 1)
            V.tensor_tensor(o_lo[:, 0:CT], pool_d[:], o_hi[:, 0:CT].bitcast(F32), ALU.subtract).then_inc(mix_ready, 1)
            dve.wait_ge(mix_out, 6)
            dve.wait_ge(lru_scan, 1)
            V.tensor_tensor(lru_h[:], lru_h[:], gelu_t[:], ALU.mult).then_inc(lru_ready, 1)
            split_lo(n + 9)
            dve.wait_ge(mix_hi, 2)
            V.tensor_tensor(o_lo[:, CT:2 * CT], lru_h[:], o_hi[:, CT:2 * CT].bitcast(F32), ALU.subtract)\
                .then_inc(mix_ready, 1)
            split_lo(n + 10)
            split_lo(n + 11)
            add_acc(4, OP_ACC, MIX_OUT + 3)
            h_input(9, 5, tabB[:, R_MLP:R_MLP + KT], None)

            H0 = DEPTH * FF_CHUNKS

            def squared(relus, chunk):
                dve.wait_ge(relu_ready, relus)
                dve.wait_ge(hid_lo_ready, chunk - 1)
                V.tensor_tensor(hid[:], silu_g[:], silu_g[:], ALU.mult).then_inc(hid_ready, 1)

            def squared_lo(chunk):
                dve.wait_ge(hid_hi_ready, chunk)
                V.tensor_tensor(hid_lo[:], hid[:], hid_hi[:].bitcast(F32), ALU.subtract).then_inc(hid_lo_ready, 1)

            n = Slab(MLP)
            split_lo(n + 2)
            squared(1, H0 + 1)
            squared_lo(H0 + 1)
            with dve.Fori(0, (UP_CHUNKS - 1) // 3) as i:
                for c3 in range(3):
                    n = Slab(MLP + 1 + 2 * c3, 6, i)
                    split_lo(n + 2)
                    squared(i * 3 + (c3 + 2), i * 3 + (H0 + c3 + 2))
                    split_lo(n + 3)
                    squared_lo(i * 3 + (H0 + c3 + 2))
            split_lo(Slab(MLP + 2 * UP_CHUNKS + 1))
            add_acc(5, FF_ACC, MLP + 2 * UP_CHUNKS - 1)
            dve.wait_ge(p_hi_ready, 1)
            V.tensor_tensor(hid_lo[:], ps[:, MISC].rearrange("p (o s) -> p o s", o=2), hid_hi[:].bitcast(F32),
                            ALU.subtract).then_inc(p_lo_ready, 1)
            split_lo(Slab(PLE_PROJ + 2))
            h_input(10, 6, tabB[:, R_PLE:R_PLE + KT], None)
            split_lo(Slab(PLE_GATE + 2))
            dve.wait_ge(proj_out, 4)
            for j in range(4):
                js = slice(2 * j, 2 * j + 2)
                dve.wait_ge(gate_out, j + 1)
                V.tensor_tensor(proj[:, js], gate[:], proj[:, js], ALU.mult).then_inc(gate_mixed, 1)
                dve.wait_ge(gate_mixed, j + 1)
                V.tensor_tensor(xt[:, js], xt[:, js], proj[:, js], ALU.add).then_inc(x_ready, 1)
                split_lo(Slab(PLE_GATE + j + 3))
            inverse_rms(11)
            for t in range(KT):
                V.scalar_tensor_tensor(out=y[:, t], in0=xt[:, t], scalar=tabB[:, R_FINAL + t:R_FINAL + t + 1],
                                       in1=rstd[:], op0=ALU.mult, op1=ALU.mult).then_inc(final_ready, 1)
            for t in range(ST):
                dve.wait_ge(final_turned, t + 3)
                V.tensor_copy(out_tok[:, t, 512:1024], ps[:, 5 + 2 * t]).then_inc(out_dve, 1)


_INS = ['x', 'c', 'rel_bias', 'ada_w', 'ada_b', 'norm_g', 'moba_w_qkv', 'moba_w_o', 'diff_w_qkv', 'diff_w_o',
        'diff_lambda', 'diff_subln_g', 'ffn_w_in', 'ffn_w_out', 'p_2', 'norm_mix_g_2', 'w_in_2', 'pool_w_2',
        'pool_b_2', 'pool_scale_2', 'conv_w_2', 'conv_b_2', 'gate_a_w_2', 'gate_a_b_2', 'gate_x_w_2',
        'gate_x_b_2', 'lru_L_2', 'w_out_2', 'norm_mlp_g_2', 'w_up_2', 'w_down_2', 'norm_ple_g_2',
        'w_ple_gate_2', 'b_ple_gate_2', 'w_ple_proj_2', 'norm_final_g_2']


def kernel(**inputs):
    import concourse.bacc as bacc
    from concourse.bass_utils import run_bass_kernel_spmd

    nc = bacc.Bacc("TRN2", target_bir_lowering=False, num_devices=1)
    arrays, args = {}, []
    for name in _INS:
        a = np.ascontiguousarray(inputs[name])
        arrays[f"in_{name}"] = a
        args.append(nc.dram_tensor(f"in_{name}", a.shape, mybir.dt.from_np(a.dtype), kind="ExternalInput").ap())
    args.append(nc.dram_tensor("out_x", (1, S, D), F32, kind="ExternalOutput").ap())
    build(nc, *args)
    return run_bass_kernel_spmd(nc, [arrays], core_ids=[0]).results[0]["out_x"]
```

```python
import math
from contextlib import ExitStack

import numpy as np
import concourse.bass as bass
from concourse import mybir

F32 = mybir.dt.float32
F32R = mybir.dt.float32r
BF16 = mybir.dt.bfloat16
ACT = mybir.ActivationFunctionType
ALU = mybir.AluOpType
AX_X = mybir.AxisListType.X

P = 128
D = 1024
KT = D // P
S = 256
ST = S // P
DEPTH = 2
HEADS = 8
HD = D // HEADS
HALF = HD // 2
D_FF = -(-8 * D // (3 * 256)) * 256
N_BUCKETS = 32
MAX_EXACT = N_BUCKETS // 2
MAX_DISTANCE = 2048
EPS = 1e-6
NEG_INF = -1e30
LAMBDA_INIT = 0.8 - 0.6 * math.exp(-0.3 * 1)
D_MIX_HALF = D // 2
CT = D_MIX_HALF // P
POOL_WINDOWS = (2, 4, 8, 16)
MAX_WINDOW = max(POOL_WINDOWS)
CONV = 4
LRU_C = 8.0
LRU_BLOCK = 64
D_FF_2 = 4 * D
PLE = 256

RING = 3
SLAB = 2048
PAIRS = HEADS // 2
FF_CHUNKS = D_FF // 256
UP_CHUNKS = D_FF_2 // 256

PER_LAYER = 3 * PAIRS + KT // 2 + 3 * FF_CHUNKS
ATTN = [l * PER_LAYER for l in range(DEPTH)]
OPROJ = [a + 3 * PAIRS for a in ATTN]
FFN = [o + KT // 2 for o in OPROJ]
MIX_IN = DEPTH * PER_LAYER
MIX_OUT = MIX_IN + 6
MLP = MIX_OUT + 4
PLE_PROJ = MLP + 2 * UP_CHUNKS
PLE_GATE = PLE_PROJ + 1
N_SLABS = PLE_GATE + 4

SH_A, SC_A, G_A, SH_F, SC_F, G_F = range(6)
ADA_RING = 3

FLIP_BANKS = [4, 5, 6, 7, 3, 2]
MISC = 3
FF_ACC = [4, 5, 6, 7]
PROJ_BANKS = [1, 2, 4, 5]
OP_ACC = [sorted({0, 1, 2, 4, 7} - {(a + 3 * PAIRS - 1) % RING}) for a in ATTN]

ROW_C = 6 * DEPTH * KT
R_NORM, R_MIX, R_MLP, R_PLE, R_FINAL, R_PLE_B, R_CONV_W, R_CONV_B, R_GA_B = 0, 64, 72, 80, 88, 96, 104, 120, 124
N_VECTORS = 14
N_LATE = 6
LRUC_STEPS = 17
R_GX_B, R_L, R_POOL_B, R_POOL_S, R_SUBLN = 0, 4, 8, 12, 16


class Slab:

    def __init__(self, first, stride=0, i=0):
        self.first, self.stride, self.i = first, stride, i

    def __add__(self, k):
        return Slab(self.first + k, self.stride, self.i)

    @property
    def place(self):
        return self.first % RING

    @property
    def turn(self):
        return self.first // RING + (self.stride // RING) * self.i if self.stride else self.first // RING

    def plus(self, k):
        return self.first + k + self.stride * self.i if self.stride else self.first + k


def bucket(n):
    if n < MAX_EXACT:
        return n
    f = np.float32
    large = MAX_EXACT + int(np.log(f(n) / f(MAX_EXACT)) / f(math.log(MAX_DISTANCE / MAX_EXACT))
                            * f(N_BUCKETS - MAX_EXACT))
    return min(large, N_BUCKETS - 1)


def bucket_runs():
    runs, j = [], 0
    while j < S:
        b, e = bucket(S - 1 - j), j
        while e < S and bucket(S - 1 - e) == b:
            e += 1
        runs.append((j, e, b))
        j = e
    return runs


def build(nc, x, c, rel_bias, ada_w, ada_b, norm_g, moba_w_qkv, moba_w_o, diff_w_qkv, diff_w_o, diff_lambda,
          diff_subln_g, ffn_w_in, ffn_w_out, p_2, norm_mix_g_2, w_in_2, pool_w_2, pool_b_2, pool_scale_2,
          conv_w_2, conv_b_2, gate_a_w_2, gate_a_b_2, gate_x_w_2, gate_x_b_2, lru_L_2, w_out_2, norm_mlp_g_2,
          w_up_2, w_down_2, norm_ple_g_2, w_ple_gate_2, b_ple_gate_2, w_ple_proj_2, norm_final_g_2, out):
    V, A, T, G = nc.vector, nc.scalar, nc.tensor, nc.gpsimd
    ds = bass.ds
    LINE = 3 * P
    line_dram = nc.dram_tensor("bias_line", (HEADS, LINE), F32, kind="Internal").ap()

    with ExitStack() as ctx:
        def sb(name, shape, dt=F32):
            return ctx.enter_context(nc.sbuf_tensor(name, shape, dt))

        def sem(name):
            return ctx.enter_context(nc.semaphore(name))

        raw = sb("raw", [P, RING, SLAB])
        w_hi = sb("w_hi", [P, RING, SLAB], F32R)
        w_lo = sb("w_lo", [P, RING, SLAB], F32R)
        ada_raw = sb("ada_raw", [P, ADA_RING, 2, D])
        ada_sum = sb("ada_sum", [P, 3, D])
        xt = sb("xt", [P, KT, S])
        y = sb("y", [P, KT, S])
        sq = sb("sq", [P, 2, 2, S])
        h_hi = sb("h_hi", [P, KT, S], F32R)
        h_lo = sb("h_lo", [P, KT, S], F32R)
        o_hi = sb("o_hi", [P, KT, S], F32R)
        o_lo = sb("o_lo", [P, KT, S], F32R)
        silu_g = sb("silu_g", [P, 2, S])
        hid = sb("hid", [P, 2, S])
        hid_hi = sb("hid_hi", [P, 2, S], F32R)
        hid_lo = sb("hid_lo", [P, 2, S], F32R)
        qkv = sb("qkv", [P, 3, 2, S])
        bias = sb("bias", [P, HEADS, LINE])
        prob = sb("prob", [P, 4, LINE])
        pt = sb("pt", [P, 2, LINE])
        tabA = sb("tabA", [P, P])
        tabB = sb("tabB", [P, P])
        tabC = sb("tabC", [P, 32])
        ident = sb("ident", [P, P])
        flip = sb("flip", [P, P])
        ones = sb("ones", [P, P])
        ones_r = sb("ones_r", [P, 2], F32R)
        zeros = sb("zeros", [P, 512], BF16)
        c_act = sb("c_act", [P, KT])
        c_pair = sb("c_pair", [P, 2])
        mods = sb("mods", [P, 12, KT])
        gain = sb("gain", [P, 4 * DEPTH, KT])
        rms = sb("rms", [P, S])
        rstd = sb("rstd", [P, S])
        rstd_tok = sb("rstd_tok", [P, ST])
        maxes = sb("maxes", [P, 2, 4])
        sums = sb("sums", [P, 2, 4])
        rsums = sb("rsums", [P, 2, 4])
        eps = sb("eps", [P, 1])
        lam_in = sb("lam_in", [P, 4, HALF])
        lam_prod = sb("lam_prod", [P, 2, HALF])
        lam_s = sb("lam_s", [P, 4])
        neg_lam = sb("neg_lam", [P, 1])
        subln = sb("subln", [P, 1])
        rel_rows = sb("rel_rows", [N_BUCKETS, HEADS])
        rel_t = sb("rel_t", [HEADS, N_BUCKETS])
        line = sb("line", [HEADS, LINE])
        inv_t = sb("inv_t", [P, MAX_WINDOW])
        lruc = sb("lruc", [P, 8, CT])

        rowsA, rowsB, rowsC = (hid[:].rearrange("p a b -> p (a b)")[:, n * P:(n + 1) * P] for n in range(3))

        def hidden_parts(chunk):
            at = slice(4 + 2 * (chunk - 1), 6 + 2 * (chunk - 1))
            return (hid_hi[:], hid_lo[:]) if chunk == 0 else (o_hi[:, at], o_lo[:, at])

        ada_hi, ada_lo = (o[:].rearrange("p a b -> p (a b)")[:, 0:D] for o in (o_hi, o_lo))

        small_w = qkv[:].rearrange("p a b c -> p (a b c)").rearrange("p (g t d) -> p g t d", g=3, t=CT)
        p_in = pt[:, :, 0:PLE]
        PADC = CONV - 1
        ul = prob[:].rearrange("p a b -> p (a b)")[:, 0:CT * (PADC + S)].rearrange("p (t s) -> p t s", t=CT)
        flat = ada_raw[:].rearrange("p a b c -> p (a b c)")
        view = lambda n: flat[:, n * CT * S:(n + 1) * CT * S].rearrange("p (t s) -> p t s", t=CT)
        xb, gate_r, gate_i, a_t, th, mult = (view(n) for n in range(6))
        bias_flat = bias[:].rearrange("p a b -> p (a b)")
        lru_h = bias_flat[:, 0:CT * S].rearrange("p (t s) -> p t s", t=CT)
        gelu_t = bias_flat[:, CT * S:2 * CT * S].rearrange("p (t s) -> p t s", t=CT)
        pool_d = bias_flat[:, 2 * CT * S:3 * CT * S].rearrange("p (t s) -> p t s", t=CT)
        PADW = MAX_WINDOW
        asum = ada_sum[:].rearrange("p a b -> p (a b)")
        win = [asum[:, n * 1280:n * 1280 + CT * (PADW + S)].rearrange("p (t s) -> p t s", t=CT) for n in range(2)]
        up = y[:].rearrange("p a b -> p (a b)")[:, 0:CT * (PADW + S)].rearrange("p (t s) -> p t s", t=CT)
        proj = bias[:].rearrange("p a b -> p (a b)")[:, 0:KT * S].rearrange("p (t s) -> p t s", t=KT)
        gate = silu_g
        out_tok = ada_raw[:, 0]
        x_tok = y[:].rearrange("p a b -> p (a b)").rearrange("p (t d) -> p t d", t=ST)

        ps = ctx.enter_context(nc.psum_tensor("ps", [P, 8, 512], F32))

        def acc(banks, t):
            return ps[:, banks[t // 2], (t % 2) * S:(t % 2) * S + S]

        slab_loaded = [sem(f"slab_loaded_{i}") for i in range(RING)]
        slab_hi, slab_lo, slab_done = sem("slab_hi"), sem("slab_lo"), sem("slab_done")
        first_mods = [sem(f"first_mods_{i}") for i in range(6)]
        ada_loaded = [sem(f"ada_loaded_{i}") for i in range(ADA_RING)]
        ada_acc, ada_reduced, mod_ready, gain_ready = (
            sem(n) for n in ("ada_acc", "ada_reduced", "mod_ready", "gain_ready"))
        c_pair_ready = sem("c_pair_ready")
        ada_hi_ready, ada_lo_ready = sem("ada_hi_ready"), sem("ada_lo_ready")
        rows_loaded, x_loaded = sem("rows_loaded"), sem("x_loaded")
        rowsA_loaded = sem("rowsA_loaded")
        ident_step, const_ready, diag_zero = sem("ident_step"), sem("const_ready"), sem("diag_zero")
        tab_turned, tab_ready, c_ready = sem("tab_turned"), sem("tab_ready"), sem("c_ready")
        rel_turned, rel_ready, line_zero, line_ready, line_stored, bias_loaded = (
            sem(n) for n in ("rel_turned", "rel_ready", "line_zero", "line_ready", "line_stored", "bias_loaded"))
        x_turned, x_ready, x_pool_ready, y_gained = (
            sem(n) for n in ("x_turned", "x_ready", "x_pool_ready", "y_gained"))
        sq_ready, sq_used, rms_ready, rstd_ready = (
            sem(n) for n in ("sq_ready", "sq_used", "rms_ready", "rstd_ready"))
        h_norm, h_hi_ready, h_ready = sem("h_norm"), sem("h_hi_ready"), sem("h_ready")
        acc_done, y_scaled = sem("acc_done"), sem("y_scaled")
        qkv_out, s_done, s_biased, s_max, s_negmax, s_exp, s_rsum, s_mixed, p_ready = (
            sem(n) for n in ("qkv_out", "s_done", "s_biased", "s_max", "s_negmax", "s_exp", "s_rsum",
                             "s_mixed", "p_ready"))
        pt_done, pt_ready, pv_done, o_hi_ready, o_ready = (
            sem(n) for n in ("pt_done", "pt_ready", "pv_done", "o_hi_ready", "o_ready"))
        head_sq, head_sum, head_rms, head_rstd, head_norm = (
            sem(n) for n in ("head_sq", "head_sum", "head_rms", "head_rstd", "head_norm"))
        silu_ready, hid_ready, hid_hi_ready, hid_lo_ready = (
            sem(n) for n in ("silu_ready", "hid_ready", "hid_hi_ready", "hid_lo_ready"))
        relu_ready = sem("relu_ready")
        lam_step, lam_exp = sem("lam_step"), sem("lam_exp")
        lruc_exp, lruc_step = sem("lruc_exp"), sem("lruc_step")
        mix_out, conv_step, gates_done, gates_out, lru_exp, lru_step, lru_mult, lru_scan = (
            sem(n) for n in ("mix_out", "conv_step", "gates_done", "gates_out", "lru_exp",
                             "lru_step", "lru_mult", "lru_scan"))
        pads_zero, pool_step, pool_done, pool_mm, pool_out, gelu_ready, lru_ready = (
            sem(n) for n in ("pads_zero", "pool_step", "pool_done", "pool_mm", "pool_out", "gelu_ready",
                             "lru_ready"))
        mix_hi, mix_ready = sem("mix_hi"), sem("mix_ready")
        p_turned, p_hi_ready, p_lo_ready = (sem(n) for n in ("p_turned", "p_hi_ready", "p_lo_ready"))
        proj_out, gate_scaled, gate_out, gate_mixed = (
            sem(n) for n in ("proj_out", "gate_scaled", "gate_out", "gate_mixed"))
        final_ready, final_turned, rms_turned, stored = (
            sem(n) for n in ("final_ready", "final_turned", "rms_turned", "stored"))
        out_act, out_dve, lru_in, inv_ready, rel_loaded, late_loaded = (
            sem(n) for n in ("out_act", "out_dve", "lru_in", "inv_ready", "rel_loaded", "late_loaded"))
        lam_loaded, bias_turned, bias_ready = sem("lam_loaded"), sem("bias_turned"), sem("bias_ready")

        def first_mod_place(m):
            if 3 <= m < 6:
                return raw[:, m - 3].rearrange("p (k n) -> p k n", k=2), first_mods[m % 6]
            return ada_raw[:, (m + 1) % ADA_RING], first_mods[m % 6]

        def wait_x(engine, update, b):
            if 1 <= update <= 4:
                if b < 2:
                    engine.wait_ge(x_pool_ready, 2 * (update - 1) + b + 1)
                else:
                    engine.wait_ge(x_ready, 2 + 2 * update + b - 1)
            else:
                engine.wait_ge(x_ready, (4 * update if update == 0 else 4 * update - 8) + b + 1)

        def cols(w, start):
            return w.rearrange("(k p) n -> p k n", p=P)[:, :, ds(start, 256)]

        def rows(w, j):
            return w.rearrange("(j k p) n -> p j k n", p=P, k=2)[:, ds(j, 1)].rearrange("p j k n -> p (j k) n")

        w_qkv = [moba_w_qkv[0], diff_w_qkv[0]]
        w_o = [moba_w_o[0], diff_w_o[0]]
        as_cols = lambda t: t.rearrange("p (k n) -> p k n", k=KT)
        as_rows = lambda t: t.rearrange("p (k n) -> p k n", k=2)

        def row_tiles(v):
            return v.rearrange("(t p) -> t p", p=P)

        block = ctx.enter_context(nc.Block())

        @block.sync
        def _(sp):
            def load(n, src, by_rows):
                if n.stride or n.first >= RING:
                    sp.wait_ge(slab_lo, n.plus(1 - RING))
                else:
                    sp.wait_ge(ada_acc, 2 * (n.first + 4))
                place = raw[:, n.place]
                sp.dma_start(as_rows(place) if by_rows else as_cols(place), src)\
                    .then_inc(slab_loaded[n.place], 16)

            sp.dma_start(rowsA[0:ROW_C, :], ada_b.rearrange("l (t p) -> (l t) p", p=P)).then_inc(rowsA_loaded, 16)
            sp.dma_start(rowsA[ROW_C:ROW_C + KT, :], row_tiles(c[0])).then_inc(rowsA_loaded, 16)
            sp.dma_start(rel_rows[:], rel_bias).then_inc(rel_loaded, 16)

            def first_mod(m):
                buffer, done = first_mod_place(m)
                if m >= 6:
                    sp.wait_ge(ada_acc, 2 * (m - 5))
                sp.dma_start(buffer, rows(ada_w[0][:, ds(m // 4 * D, D)], m % 4)).then_inc(done, 16)

            first_mod(0)
            first_mod(1)
            sp.dma_start(x_tok, x[0].rearrange("(t p) d -> p t d", p=P)).then_inc(x_loaded, 16)
            for m in range(2, 6):
                first_mod(m)
            vectors = (
                (rowsB, R_NORM, 4 * DEPTH * KT, norm_g.rearrange("l n (t p) -> (l n t) p", p=P)),
                (rowsB, R_MIX, KT, row_tiles(norm_mix_g_2[0])), (rowsB, R_MLP, KT, row_tiles(norm_mlp_g_2[0])),
                (rowsB, R_PLE, KT, row_tiles(norm_ple_g_2[0])), (rowsB, R_FINAL, KT, row_tiles(norm_final_g_2)),
                (rowsB, R_PLE_B, KT, row_tiles(b_ple_gate_2[0])),
                (rowsB, R_CONV_W, CONV * CT, conv_w_2[0].rearrange("k (t p) -> (k t) p", p=P)),
                (rowsB, R_CONV_B, CT, row_tiles(conv_b_2[0])),
                (rowsB, R_GA_B, CT, gate_a_b_2[0].rearrange("(t h) d -> t (h d)", h=2)),
                (rowsC, R_GX_B, CT, gate_x_b_2[0].rearrange("(t h) d -> t (h d)", h=2)),
                (rowsC, R_L, CT, row_tiles(lru_L_2[0])), (rowsC, R_POOL_B, CT, pool_b_2[0]),
                (rowsC, R_POOL_S, CT, row_tiles(pool_scale_2[0])), (rowsC, R_SUBLN, 1, diff_subln_g),
            )
            assert len(vectors) == N_VECTORS
            for dst, r, n, src in vectors:
                sp.dma_start(dst[r:r + n, :], src).then_inc(rows_loaded, 16)
            first_mod(6)
            first_mod(7)
            for l in range(DEPTH):
                for t in range(3):
                    load(Slab(ATTN[l] + t), cols(w_qkv[l], t * D), False)
                with sp.Fori(1, PAIRS) as j:
                    for t in range(3):
                        load(Slab(ATTN[l] + t, 3, j), cols(w_qkv[l], j * 256 + t * D), False)
                for j in range(KT // 2):
                    load(Slab(OPROJ[l] + j), rows(w_o[l], j), True)
                load(Slab(FFN[l]), cols(ffn_w_in[l], 0), False)
                load(Slab(FFN[l] + 1), cols(ffn_w_in[l], D_FF), False)
                with sp.Fori(0, FF_CHUNKS - 1) as j:
                    n = Slab(FFN[l] + 2, 3, j)
                    load(n, cols(ffn_w_in[l], j * 256 + 256), False)
                    load(n + 1, cols(ffn_w_in[l], j * 256 + (D_FF + 256)), False)
                    load(n + 2, rows(ffn_w_out[l], j), True)
                load(Slab(FFN[l] + 3 * FF_CHUNKS - 1), rows(ffn_w_out[l], FF_CHUNKS - 1), True)
                if l == 0:
                    sp.dma_start(lam_in[:], bass.AP(diff_lambda.tensor, 0, [[0, P], [HALF, 4], [1, HALF]]))\
                        .then_inc(lam_loaded, 16)
            sp.wait_ge(diag_zero, 1)
            late = [(p_in, p_2[0, 0].rearrange("(t p) d -> p t d", p=P)),
                    (small_w[:, 2], pool_w_2[0].rearrange("g c d -> c g d"))]
            for g, w in enumerate((gate_a_w_2, gate_x_w_2)):
                for hh in range(2):
                    at = slice(hh * LRU_BLOCK, (hh + 1) * LRU_BLOCK)
                    late.append((small_w[at, g, :, at], w[0].rearrange("(t h) i j -> h i t j", h=2)[hh]))
            assert len(late) == N_LATE
            for dst, src in late:
                sp.dma_start(dst, src).then_inc(late_loaded, 16)
            for s, col in enumerate((512, 768, 0, 256, 1024, 1280)):
                load(Slab(MIX_IN + s), cols(w_in_2[0], col), False)
            for j in range(KT // 2):
                load(Slab(MIX_OUT + j), rows(w_out_2[0], j), True)
            load(Slab(MLP), cols(w_up_2[0], 0), False)
            with sp.Fori(0, (UP_CHUNKS - 1) // 3) as i:
                for c3 in range(3):
                    n = Slab(MLP + 1 + 2 * c3, 6, i)
                    load(n, cols(w_up_2[0], i * 768 + 256 * (c3 + 1)), False)
                    load(n + 1, rows(w_down_2[0], i * 3 + c3), True)
            load(Slab(MLP + 2 * UP_CHUNKS - 1), rows(w_down_2[0], UP_CHUNKS - 1), True)
            load(Slab(PLE_PROJ), rows(w_ple_proj_2[0], 0), True)
            for j in range(4):
                load(Slab(PLE_GATE + j), cols(w_ple_gate_2[0], 256 * j), False)
            for t in range(ST):
                sp.wait_ge(out_act, t + 1)
                sp.wait_ge(out_dve, t + 1)
                sp.dma_start(out[0, t * P:(t + 1) * P, :], out_tok[:, t]).then_inc(stored, 16)
            sp.wait_ge(stored, 16 * ST)

        @block.gpsimd
        def _(pool):
            def load_ada(l, kp, col, place, need):
                pool.wait_ge(ada_acc, need)
                pool.dma_start(ada_raw[:, place], rows(ada_w[l][:, ds(col, D)], kp)).then_inc(ada_loaded[place], 16)

            G.memset(ident[:], 0.0).then_inc(ident_step, 1)
            pool.wait_ge(ident_step, 1)
            G.affine_select(out=ident[:], in_=ident[:], compare_op=ALU.not_equal, fill=1.0, base=0,
                            pattern=[[-1, P]], channel_multiplier=1).then_inc(ident_step, 1)
            G.memset(flip[:], 0.0).then_inc(ident_step, 1)
            pool.wait_ge(ident_step, 3)
            G.affine_select(out=flip[:], in_=flip[:], compare_op=ALU.not_equal, fill=1.0, base=1 - P,
                            pattern=[[1, P]], channel_multiplier=1).then_inc(ident_step, 1)
            G.memset(line[:], NEG_INF).then_inc(line_zero, 1)
            pool.wait_ge(line_zero, 1)
            pool.wait_ge(rel_ready, 1)
            for a, b, k in bucket_runs():
                last = G.tensor_copy(line[:, a:b], rel_t[:, k:k + 1].to_broadcast([HEADS, b - a]))
            last.then_inc(line_ready, 1)
            pool.wait_ge(line_ready, 1)
            pool.dma_start(line_dram, line[:]).then_inc(line_stored, 16)
            pool.wait_ge(line_stored, 16)
            for first, at, width in ((0, 0, S), (P, S, P)):
                src = bass.AP(line_dram.tensor, first, [[1, P], [LINE, HEADS], [1, width]])
                pool.dma_start(bias[:, :, at:at + width], src).then_inc(bias_loaded, 16)
            for t in range(MAX_WINDOW):
                last = G.memset(inv_t[:, t:t + 1], 1.0 / (t + 1))
            last.then_inc(inv_ready, 1)
            with pool.Fori(0, PAIRS) as j:
                for c3 in range(3):
                    load_ada(0, j, (G_A + c3) * D, c3, j * 6 + 2 * (8 + c3 - 2))
            def add_y_pairs(i):
                for b in range(2):
                    pair = slice(2 * b, 2 * b + 2)
                    pool.wait_ge(y_scaled, 4 * i + b + 1)
                    G.tensor_tensor(xt[:, pair], xt[:, pair], y[:, pair], ALU.add).then_inc(x_pool_ready, 1)

            for m in range(20, 24):
                load_ada(0, m % 4, G_F * D, (m + 1) % 3, 2 * (m - 2))
            add_y_pairs(0)
            with pool.Fori(0, 5) as i:
                for kp in range(4):
                    load_ada(1, kp, i * D, (kp + 1) % 2, i * 8 + 2 * (24 + kp - 1))
            add_y_pairs(1)
            with pool.Fori(0, PAIRS) as j:
                load_ada(1, j, G_F * D, 2, j * 2 + 2 * 44)
            pool.wait_ge(o_ready, DEPTH * PAIRS)
            G.memset(qkv[:], 0.0).then_inc(diag_zero, 1)
            add_y_pairs(2)
            add_y_pairs(3)

        @block.tensor
        def _(pe):
            def three(out_ap, hi_s, lo_s, hi_m, lo_m, start, stop):
                T.matmul(out_ap, hi_s, hi_m, start=start, stop=False, skip_group_check=True)
                T.matmul(out_ap, hi_s, lo_m, start=False, stop=False, skip_group_check=True)
                return T.matmul(out_ap, lo_s, hi_m, start=False, stop=stop, skip_group_check=True)

            def col_slab(n, h_base=None, norm=None):
                pe.wait_ge(slab_lo, n.plus(1))
                wh, wl = as_cols(w_hi[:, n.place]), as_cols(w_lo[:, n.place])
                for k in range(KT):
                    if h_base is not None:
                        pe.wait_ge(h_ready, h_base + k + 1)
                    for o in range(2):
                        cs = slice(o * P, o * P + P)
                        last = three(ps[:, n.place, o * S:(o + 1) * S], wh[:, k, cs], wl[:, k, cs],
                                     h_hi[:, k], h_lo[:, k], k == 0 and o == 0, k == KT - 1)
                    if k == KT - 1:
                        last.then_inc(slab_done, 1)
                    if norm is not None and k in (3, 5, 7):
                        sum_pair(norm, (k - 3) // 2, y)
                if norm is not None:
                    sum_pair(norm, 3, y)

            def v_slab(n):
                pe.wait_ge(slab_lo, n.plus(1))
                wh, wl = as_cols(w_hi[:, n.place]), as_cols(w_lo[:, n.place])
                for k in range(KT):
                    for t in range(ST):
                        ts = slice(t * P, t * P + P)
                        last = three(ps[:, n.place, t * 256:(t + 1) * 256], h_hi[:, k, ts], h_lo[:, k, ts],
                                     wh[:, k], wl[:, k], k == 0 and t == 0, k == KT - 1)
                last.then_inc(slab_done, 1)

            def row_slab(n, banks, hi, lo, first, final, norm=None, meanwhile=None):
                pe.wait_ge(slab_lo, n.plus(1))
                wh, wl = as_rows(w_hi[:, n.place]), as_rows(w_lo[:, n.place])
                for t in range(KT):
                    cs = slice(t * P, t * P + P)
                    for k in range(2):
                        last = three(acc(banks, t), wh[:, k, cs], wl[:, k, cs], hi[:, k], lo[:, k],
                                     first and k == 0 and t % 2 == 0, final and k == 1)
                    if meanwhile:
                        meanwhile(t)
                    if final and t % 2 == 1 and t < KT - 1:
                        last.then_inc(acc_done, 1)
                        if norm is not None and t > 1:
                            sum_pair(norm, t // 2 - 1)
                last.then_inc(slab_done, 1)
                if norm is not None:
                    sum_pair(norm, 2)
                    sum_pair(norm, 3)

            def sum_pair(norm, b, squares=None):
                pe.wait_ge(sq_ready, 4 * norm + b + 1)
                for o in range(2):
                    tile = sq[:, b % 2, o] if squares is None else squares[:, 2 * b + o]
                    last = T.matmul(ps[:, MISC, 0:S], ones[:], tile, start=b == 0 and o == 0,
                                    stop=b == 3 and o == 1, skip_group_check=True)
                last.then_inc(sq_used, 1)

            def sum_squares(norm):
                for b in range(KT // 2):
                    sum_pair(norm, b)

            def reduce_mods(bank, slots, first=0):
                for s in range(first, slots):
                    for t in range(KT):
                        last = T.matmul(ps[:, bank, s * KT + t:s * KT + t + 1], ada_sum[:, s, t * P:(t + 1) * P],
                                        ones[:, 0:1], start=True, stop=True)
                last.then_inc(ada_reduced, 1)

            def clear_acc(banks):
                for b in banks:
                    T.matmul(ps[:, b], zeros[:, 0:P], zeros[:], start=True, stop=True, skip_group_check=True)

            def keep_warm(bank, n):
                for _ in range(n):
                    T.matmul(ps[:, bank], zeros[:, 0:P], zeros[:], start=True, stop=True, skip_group_check=True)

            pe.wait_ge(ident_step, 2)
            pe.wait_ge(rowsA_loaded, 32)
            T.transpose(ps[:, 0, 0:ROW_C + KT], rowsA[0:ROW_C + KT, :], ident[0:ROW_C + KT, 0:ROW_C + KT])\
                .then_inc(tab_turned, 1)
            pe.wait_ge(rel_loaded, 16)
            T.transpose(ps[0:HEADS, 1, 0:N_BUCKETS], rel_rows[:], ident[0:N_BUCKETS, 0:N_BUCKETS])\
                .then_inc(rel_turned, 1)
            pe.wait_ge(x_loaded, 16)
            for b in range(4):
                for o in range(2):
                    for t in range(ST):
                        f = 2 * b + o
                        last = T.transpose(ps[:, 4 + b, o * S + t * P:o * S + (t + 1) * P],
                                           x_tok[:, t, f * P:(f + 1) * P], ident[:])
                last.then_inc(x_turned, 1)
            pe.wait_ge(rows_loaded, 16 * N_VECTORS)
            T.transpose(ps[:, 2, 0:P], rowsB, ident[:]).then_inc(tab_turned, 1)
            pe.wait_ge(tab_ready, 1)
            T.transpose(ps[:, 0, 0:R_SUBLN + 1], rowsC[0:R_SUBLN + 1, :], ident[0:R_SUBLN + 1, 0:R_SUBLN + 1])\
                .then_inc(tab_turned, 1)
            pe.wait_ge(const_ready, 3)
            sum_squares(0)
            pe.wait_ge(rel_ready, 1)
            pe.wait_ge(ada_acc, 2 * 4)
            reduce_mods(1, 1)
            pe.wait_ge(tab_ready, 3)
            pe.wait_ge(ada_acc, 2 * 8)
            reduce_mods(0, 2, 1)
            pe.wait_ge(ident_step, 4)
            pe.wait_ge(bias_loaded, 32)
            pe.wait_ge(x_ready, 4)
            pe.wait_ge(rms_ready, 1)

            def flip_bias(blocks):
                for b in blocks:
                    T.matmul(ps[:, FLIP_BANKS[b]], flip[:], bias_flat[:, b * 512:(b + 1) * 512], start=True,
                             stop=True).then_inc(bias_turned, 1)

            flip_bias(range(3))

            for l in range(DEPTH):
                units = 1 + l

                def turn_probs(pairs, banks):
                    pe.wait_ge(p_ready, pairs)
                    for hh in range(2):
                        u, b = hh * units, banks[hh]
                        T.transpose(ps[:, b, 0:P], prob[:, u, S:S + P], ident[:])
                        T.transpose(ps[:, b, P:2 * P], prob[:, u, 0:P], ident[:])
                        last = T.transpose(ps[:, b, 2 * P:3 * P], prob[:, u, P:2 * P], ident[:])
                    last.then_inc(pt_done, 1)

                def attend(pairs):
                    pe.wait_ge(qkv_out, pairs * 3)
                    v = qkv[:, 2]
                    pe.wait_ge(pt_ready, pairs)
                    for hh in range(2):
                        hs = slice(hh * HD, hh * HD + HD)
                        T.matmul(ps[:, MISC, hh * S:(hh + 1) * S], v[:, 0, hs], pt[:, hh, 0:S],
                                 start=True, stop=False, skip_group_check=True)
                        last = T.matmul(ps[:, MISC, hh * S + P:(hh + 1) * S], v[:, 1, hs], pt[:, hh, S:S + P],
                                        start=False, stop=True, skip_group_check=True)
                    last.then_inc(pv_done, 1)

                def head_squares(pairs):
                    pe.wait_ge(head_sq, pairs)
                    T.matmul(ps[:, MISC], ones[:], silu_g[:].rearrange("p a b -> p (a b)"), start=True, stop=True)\
                        .then_inc(head_sum, 1)

                def scores(need):
                    pe.wait_ge(qkv_out, need)
                    q, k = qkv[:, 0], qkv[:, 1]
                    for hh in range(2):
                        for cc in range(units):
                            if l == 0:
                                rs = slice(0, P)
                                late, early = ps[:, 4, hh * S:(hh + 1) * S], ps[:, 5, hh * P:(hh + 1) * P]
                            else:
                                rs = slice(cc * HALF, (cc + 1) * HALF)
                                late = ps[:, 4 + cc, hh * S:(hh + 1) * S]
                                early = ps[:, 6 + cc, hh * P:(hh + 1) * P]
                            T.matmul(late, q[rs, hh, P:S], k[rs, hh, :], start=True, stop=True)
                            last = T.matmul(early, q[rs, hh, 0:P], k[rs, hh, 0:P], start=True, stop=True)
                    last.then_inc(s_done, 1)

                def pair(j, n, first):
                    pairs = j + PAIRS * l
                    col_slab(n, 8 * 2 * l if first else None)
                    col_slab(n + 1)
                    if not first:
                        pe.wait_ge(qkv_out, pairs * 3 + 1)
                        turn_probs(pairs, sorted((n.place, (n + 2).place)))
                    elif l == 0:
                        flip_bias(range(3, 6))
                        pe.wait_ge(bias_ready, 6)
                    scores(pairs * 3 + 2)
                    if not first:
                        attend(pairs)
                    if l and not first:
                        head_squares(j)
                    v_slab(n + 2)

                pair(0, Slab(ATTN[l]), True)
                with pe.Fori(1, PAIRS) as j:
                    pair(j, Slab(ATTN[l], 3, j), False)
                pairs = PAIRS * (l + 1)
                pe.wait_ge(s_biased, pairs)
                for j in range(KT // 2):
                    if j == 2:
                        turn_probs(pairs, (5, 6))
                        attend(pairs)
                        if l == 0:
                            pe.wait_ge(ada_acc, 2 * 20)
                            reduce_mods(5, 3)
                        else:
                            pe.wait_ge(ada_acc, 2 * 48)
                            reduce_mods(5, 1)
                            head_squares(PAIRS)
                    pe.wait_ge(o_ready, PAIRS * l + j + 1)
                    js = slice(2 * j, 2 * j + 2)
                    row_slab(Slab(OPROJ[l] + j), OP_ACC[l], o_hi[:, js], o_lo[:, js], j == 0, j == 3,
                             1 + 4 * l if j == 3 else None)
                keep_warm(6, 20)
                sum_squares(2 + 4 * l)
                pe.wait_ge(y_gained, 4 * (2 * l + 1))
                clear_acc(FF_ACC)

                def reduce_tile(t):
                    ts, to = slice(t * P, (t + 1) * P), ps[:, MISC, 2 * t:2 * t + 2]
                    T.matmul(to, ada_hi[:, ts], ones_r[:], start=True, stop=False, skip_group_check=True)
                    last = T.matmul(to, ada_lo[:, ts], ones_r[:], start=False, stop=True, skip_group_check=True)
                    if t == KT - 1:
                        last.then_inc(ada_reduced, 1)

                def down(n, chunks, parts, final=False, meanwhile=None):
                    pe.wait_ge(hid_lo_ready, chunks)
                    row_slab(n, FF_ACC, *hidden_parts(parts), False, final, 3 + 4 * l if final else None,
                             meanwhile)

                col_slab(Slab(FFN[l]), 8 * (2 * l + 1))
                col_slab(Slab(FFN[l] + 1))
                if l == 0:
                    pe.wait_ge(ada_acc, 2 * 24)
                    reduce_mods(MISC, 1)
                with pe.Fori(0, (FF_CHUNKS - 1) // 2) as i:
                    for c2 in range(2):
                        n = Slab(FFN[l] + 2 + 3 * c2, 6, i)
                        pe.wait_ge(hid_ready, i * 2 + (FF_CHUNKS * l + c2 + 1))
                        col_slab(n)
                        col_slab(n + 1)
                        if l == 0 and c2 == 1:
                            pe.wait_ge(ada_lo_ready, i + 1)
                            pe.wait_ge(mod_ready, i + 6)
                        down(n + 2, i * 2 + (FF_CHUNKS * l + c2 + 1), c2, False,
                             reduce_tile if l == 0 and c2 == 1 else None)
                if l == 0:
                    pe.wait_ge(mod_ready, 11)
                down(Slab(FFN[l] + 3 * FF_CHUNKS - 1), FF_CHUNKS * (l + 1), 0, True)
                keep_warm(Slab(FFN[l] + 3 * FF_CHUNKS).place, 20)
                if l == 0:
                    sum_squares(4)

            hb = 8 * 4
            for s in range(4):
                if s == 3:
                    pe.wait_ge(mix_out, 1)
                col_slab(Slab(MIX_IN + s), hb if s == 0 else None, 8 if s == 0 else None)
            pe.wait_ge(conv_step, 4 * CONV)
            pe.wait_ge(late_loaded, 16 * N_LATE)
            pe.wait_ge(y_gained, 16)
            for g in range(2):
                for t in range(CT):
                    last = T.matmul(ps[:, 4 + 2 * g + t // 2, (t % 2) * S:(t % 2) * S + S], small_w[:, g, t],
                                    xb[:, t], start=True, stop=True)
                last.then_inc(gates_done, 1)
            pe.wait_ge(mix_out, 2)
            col_slab(Slab(MIX_IN + 4))
            pe.wait_ge(pool_done, 1)
            pe.wait_ge(gates_out, 2)
            for t in range(CT):
                last = T.matmul(ps[:, 4 + t // 2, (t % 2) * S:(t % 2) * S + S], small_w[:, 2, t], pool_d[:, t],
                                start=True, stop=True)
            last.then_inc(pool_mm, 1)
            pe.wait_ge(mix_out, 3)
            col_slab(Slab(MIX_IN + 5))
            pe.wait_ge(gates_out, 4)
            for j in range(KT // 2):
                pe.wait_ge(mix_ready, j // 2 + 1)
                js = slice(2 * j, 2 * j + 2)
                row_slab(Slab(MIX_OUT + j), FF_ACC, o_hi[:, js], o_lo[:, js], j == 0, j == 3)

            H0 = DEPTH * FF_CHUNKS
            col_slab(Slab(MLP), 8 * 5, 9)
            wait_x(pe, 5, 3)
            clear_acc(FF_ACC)
            with pe.Fori(0, (UP_CHUNKS - 1) // 3) as i:
                for c3 in range(3):
                    n = Slab(MLP + 1 + 2 * c3, 6, i)
                    pe.wait_ge(relu_ready, i * 3 + (c3 + 1))
                    col_slab(n)
                    pe.wait_ge(hid_lo_ready, i * 3 + (H0 + c3 + 1))
                    row_slab(n + 1, FF_ACC, *hidden_parts(c3), False, False)
            for o in range(2):
                for t in range(ST):
                    last = T.transpose(ps[:, MISC, o * S + t * P:o * S + (t + 1) * P], p_in[:, t, o * P:(o + 1) * P],
                                       ident[:])
            last.then_inc(p_turned, 1)
            pe.wait_ge(hid_lo_ready, H0 + UP_CHUNKS)
            row_slab(Slab(MLP + 2 * UP_CHUNKS - 1), FF_ACC, *hidden_parts(0), False, True)
            pe.wait_ge(p_lo_ready, 1)
            wait_x(pe, 6, 1)
            row_slab(Slab(PLE_PROJ), PROJ_BANKS, o_hi[:, 0:2], o_lo[:, 0:2], True, True)
            def finish_pair(b):
                if b == 0:
                    pe.wait_ge(rms_ready, 11)
                sum_pair(11, b)
                pe.wait_ge(final_ready, b + 1)
                for t in range(ST):
                    for f in range(2 * b, 2 * b + 2):
                        last = T.transpose(ps[:, 4 + 2 * t + f // 4, f % 4 * P:(f % 4 + 1) * P],
                                           y[:, f, t * P:(t + 1) * P], ident[:])
                last.then_inc(final_turned, 1)

            for j in range(4):
                if j == 1:
                    pe.wait_ge(proj_out, 4)
                if j == 3:
                    pe.wait_ge(gate_scaled, 1)
                col_slab(Slab(PLE_GATE + j), 8 * 6 if j == 0 else None, 10 if j == 0 else None)
                if j == 2:
                    finish_pair(0)
                if j > 1:
                    finish_pair(j - 1)
            finish_pair(3)
            pe.wait_ge(rms_ready, 12)
            for t in range(ST):
                last = T.matmul(ps[:, MISC, S + t:S + t + 1], rms[:, t * P:(t + 1) * P], ident[:, 0:1], start=True,
                                stop=True)
            last.then_inc(rms_turned, 1)

        @block.scalar
        def _(act):
            def split_hi(n):
                if n.first >= N_SLABS:
                    return
                act.wait_ge(slab_loaded[n.place], n.turn * 16 + 16)
                if n.stride or n.first >= RING:
                    act.wait_ge(slab_done, n.plus(1 - RING))
                A.activation(w_hi[:, n.place], raw[:, n.place], ACT.Copy).then_inc(slab_hi, 1)

            def norm(k, src, wait, after=None):
                A.preload_act_table(ACT.Sqrt)
                for b in range(KT // 2):
                    wait(b)
                    if 4 * k + b >= 2:
                        act.wait_ge(sq_used, 4 * k + b - 1)
                    A.activation(sq[:, b % 2], src(b), ACT.Square).then_inc(sq_ready, 1)
                    if after:
                        after(b)
                act.wait_ge(sq_used, 4 * k + 4)
                A.activation(rms[:], ps[:, MISC, 0:S], ACT.Sqrt, bias=eps[:, 0:1], scale=1.0 / D)\
                    .then_inc(rms_ready, 1)

            def norm_x(k, update):
                norm(k, lambda b: xt[:, 2 * b:2 * b + 2], lambda b: wait_x(act, update, b))

            def norm_y(k, i, banks, slab, gains, gains_done):
                def gained(b):
                    if b == 0:
                        act.wait_ge(gain_ready, gains_done)
                    for t in (2 * b, 2 * b + 1):
                        last = A.activation(y[:, t], acc(banks, t), ACT.Copy, scale=gains[:, t:t + 1])
                    last.then_inc(y_gained, 1)

                def complete(b):
                    if b < 3:
                        act.wait_ge(acc_done, 3 * i + b + 1)
                    else:
                        act.wait_ge(slab_done, slab + 1)
                norm(k, lambda b: ps[:, banks[b]].rearrange("p (o s) -> p o s", o=2), complete, gained)

            def raw_input(k, update, i, gains, ahead, before_root=None):
                for b in range(KT // 2):
                    wait_x(act, update, b)
                    for t in (2 * b, 2 * b + 1):
                        A.activation(h_hi[:, t], xt[:, t], ACT.Copy, scale=gains[:, t:t + 1]).then_inc(h_hi_ready, 1)
                    pair = slice(2 * b, 2 * b + 2)
                    A.activation(y[:, pair], xt[:, pair], ACT.Square).then_inc(sq_ready, 1)
                split_hi(ahead)
                if before_root:
                    before_root()
                A.preload_act_table(ACT.Sqrt)
                act.wait_ge(sq_used, 4 * k + 4)
                A.activation(rms[:], ps[:, MISC, 0:S], ACT.Sqrt, bias=eps[:, 0:1], scale=1.0 / D)\
                    .then_inc(rms_ready, 1)

            def h_high(i, shift, between=None):
                for t in range(KT):
                    if between and t == 4:
                        split_hi(between)
                    act.wait_ge(h_norm, 8 * i + t + 1)
                    if shift is None:
                        A.activation(h_hi[:, t], y[:, t], ACT.Copy).then_inc(h_hi_ready, 1)
                    else:
                        A.activation(h_hi[:, t], y[:, t], ACT.Identity, bias=mods[:, shift, t:t + 1])\
                            .then_inc(h_hi_ready, 1)

            act.wait_ge(tab_ready, 1)
            A.activation(c_act[:], tabA[:, ROW_C:ROW_C + KT], ACT.Silu).then_inc(c_ready, 1)
            for b in range(4):
                act.wait_ge(x_turned, b + 1)
                A.activation(xt[:, 2 * b:2 * b + 2], ps[:, 4 + b], ACT.Copy).then_inc(x_ready, 1)
            act.wait_ge(const_ready, 3)
            A.activation(ones_r[:], ones[:, 0:2], ACT.Copy)
            norm_x(0, 0)
            split_hi(Slab(0))
            h_high(0, SH_A, Slab(1))

            def bias_out(blocks):
                for b in blocks:
                    act.wait_ge(bias_turned, b + 1)
                    A.activation(bias_flat[:, b * 512:(b + 1) * 512], ps[:, FLIP_BANKS[b]], ACT.Copy)\
                        .then_inc(bias_ready, 1)

            bias_out(range(3))

            for l in range(DEPTH):
                units = 1 + l

                def exps(pairs):
                    act.wait_ge(s_negmax, pairs)
                    for u in range(2 * units):
                        A.activation(prob[:, u, 0:S], prob[:, u, 0:S], ACT.Exp, bias=maxes[:, 0, u:u + 1],
                                     accum_out=sums[:, 0, u:u + 1])
                        last = A.activation(prob[:, u, S:S + P], prob[:, u, S:S + P], ACT.Exp,
                                            bias=maxes[:, 1, u:u + 1], accum_out=sums[:, 1, u:u + 1])
                    last.then_inc(s_exp, 1)

                def copy_turned(pairs, banks):
                    act.wait_ge(pt_done, pairs)
                    both = slice(banks[0], banks[1] + 1, banks[1] - banks[0])
                    A.activation(pt[:], ps[:, both, 0:LINE], ACT.Copy).then_inc(pt_ready, 1)

                def heads_out(pairs, at):
                    act.wait_ge(pv_done, pairs)
                    if l == 0:
                        A.activation(o_hi[:, at], ps[:, MISC], ACT.Copy).then_inc(o_hi_ready, 1)
                    else:
                        act.wait_ge(o_ready, pairs - 1)
                        A.activation(hid[:], ps[:, MISC], ACT.Copy)
                        A.activation(silu_g[:], ps[:, MISC], ACT.Square).then_inc(head_sq, 1)

                def heads_rms(j):
                    act.wait_ge(head_sum, j)
                    A.activation(sq[:, 0], ps[:, MISC], ACT.Sqrt, bias=eps[:, 0:1], scale=1.0 / HD)\
                        .then_inc(head_rms, 1)

                def heads_hi(j, at):
                    act.wait_ge(head_norm, j)
                    A.activation(o_hi[:, at], hid[:], ACT.Copy).then_inc(o_hi_ready, 1)

                def pair(j, n, first):
                    pairs = j + PAIRS * l
                    split_hi(n + 2)
                    act.wait_ge(slab_done, n.plus(1))
                    A.activation(qkv[:, 0], ps[:, n.place], ACT.Copy, scale=(HALF if l else HD) ** -0.5)\
                        .then_inc(qkv_out, 1)
                    split_hi(n + 3)
                    act.wait_ge(slab_done, n.plus(2))
                    A.activation(qkv[:, 1], ps[:, (n + 1).place], ACT.Copy).then_inc(qkv_out, 1)
                    if l == 0 and first:
                        bias_out(range(3, 6))
                    if not first:
                        copy_turned(pairs, sorted((n.place, (n + 2).place)))
                        heads_out(pairs, ds(2 * j - 2, 2))
                    split_hi(n + 4)
                    if l and not first:
                        heads_rms(j)
                    exps(pairs + 1)
                    act.wait_ge(slab_done, n.plus(3))
                    A.activation(qkv[:, 2], ps[:, (n + 2).place], ACT.Copy).then_inc(qkv_out, 1)
                    if l and not first:
                        heads_hi(j, ds(2 * j - 2, 2))

                pair(0, Slab(ATTN[l]), True)
                with act.Fori(1, PAIRS) as j:
                    pair(j, Slab(ATTN[l], 3, j), False)
                pairs = PAIRS * (l + 1)
                n = Slab(OPROJ[l])
                split_hi(n + 2)
                split_hi(n + 3)
                copy_turned(pairs, (5, 6))
                heads_out(pairs, slice(6, 8))
                if l:
                    heads_rms(PAIRS)
                    heads_hi(PAIRS, slice(6, 8))
                split_hi(n + 4)
                split_hi(n + 5)
                norm_y(1 + 4 * l, 2 * l, OP_ACC[l], OPROJ[l] + 3, gain[:, 4 * l + 1], 2 + 4 * l)
                norm_x(2 + 4 * l, 2 * l + 1)
                h_high(2 * l + 1, 6 * l + SH_F)

                def gated(n):
                    act.wait_ge(slab_done, n.plus(1))
                    A.activation(silu_g[:], ps[:, n.place], ACT.Silu).then_inc(silu_ready, 1)

                def hidden_hi(chunk, parts):
                    act.wait_ge(hid_ready, chunk)
                    A.activation(hidden_parts(parts)[0], hid[:], ACT.Copy).then_inc(hid_hi_ready, 1)

                A.preload_act_table(ACT.Silu)
                n = Slab(FFN[l])
                split_hi(n + 2)
                gated(n)
                split_hi(n + 3)
                hidden_hi(FF_CHUNKS * l + 1, 0)
                with act.Fori(0, (FF_CHUNKS - 1) // 2) as i:
                    for c2 in range(2):
                        n = Slab(FFN[l] + 2 + 3 * c2, 6, i)
                        split_hi(n + 2)
                        gated(n)
                        split_hi(n + 3)
                        if l == 0 and c2 == 1:
                            act.wait_ge(ada_acc, i * 8 + 2 * 28)
                            act.wait_ge(ada_reduced, i + 4)
                            A.activation(ada_hi, ada_sum[:, 0], ACT.Copy).then_inc(ada_hi_ready, 1)
                        split_hi(n + 4)
                        hidden_hi(i * 2 + (FF_CHUNKS * l + c2 + 2), 1 - c2)
                split_hi(Slab(FFN[l] + 3 * FF_CHUNKS + 1))
                norm_y(3 + 4 * l, 2 * l + 1, FF_ACC, FFN[l] + 3 * FF_CHUNKS - 1, gain[:, 4 * l + 3], 4 + 4 * l)
                if l == 0:
                    norm_x(4, 2)
                    h_high(2, 6 + SH_A)
                    act.wait_ge(lam_step, 2)
                    A.activation(lam_s[:, 2:4], lam_s[:, 0:2], ACT.Exp).then_inc(lam_exp, 1)
                    act.wait_ge(lruc_step, 2)
                    A.activation(lruc[:, 2], lruc[:, 1], ACT.Exp).then_inc(lruc_exp, 1)

            n = Slab(MIX_IN)

            raw_input(8, 4, 4, tabB[:, R_MIX:R_MIX + KT], n + 2)
            for s in range(3, 7):
                split_hi(n + s)
            for g, dst in enumerate((gate_r, gate_i)):
                act.wait_ge(gates_done, g + 1)
                for t in range(CT):
                    b = tabB[:, R_GA_B + t:R_GA_B + t + 1] if g == 0 else tabC[:, R_GX_B + t:R_GX_B + t + 1]
                    last = A.activation(dst[:, t], ps[:, 4 + 2 * g + t // 2, (t % 2) * S:(t % 2) * S + S],
                                        ACT.Sigmoid, bias=b)
                    if t % 2 == 1:
                        last.then_inc(gates_out, 1)
            act.wait_ge(gates_out, 2)
            act.wait_ge(lruc_step, LRUC_STEPS)
            for t in range(CT):
                A.activation(a_t[:, t], gate_r[:, t], ACT.Exp, scale=lruc[:, 7, t:t + 1])
                last = A.activation(th[:, t], gate_r[:, t], ACT.Tanh, scale=lruc[:, 7, t:t + 1])
            last.then_inc(lru_exp, 1)
            split_hi(n + 7)
            act.wait_ge(lru_step, 2)
            A.activation(mult[:], th[:], ACT.Sqrt, scale=-1.0).then_inc(lru_mult, 1)
            act.wait_ge(pool_out, 1)
            A.activation(o_hi[:, 0:CT], pool_d[:], ACT.Copy).then_inc(mix_hi, 1)
            split_hi(n + 8)
            for half in range(2):
                act.wait_ge(mix_out, 5 + half)
                g2 = gelu_t[:, 2 * half:2 * half + 2]
                A.activation(g2, g2, ACT.Gelu_apprx_tanh).then_inc(gelu_ready, 1)
            act.wait_ge(lru_ready, 1)
            A.activation(o_hi[:, CT:2 * CT], lru_h[:], ACT.Copy).then_inc(mix_hi, 1)
            split_hi(n + 9)
            split_hi(n + 10)
            split_hi(n + 11)
            raw_input(9, 5, 5, tabB[:, R_MLP:R_MLP + KT], Slab(MLP + 2))

            H0 = DEPTH * FF_CHUNKS

            def squared(chunk, parts):
                act.wait_ge(relu_ready, chunk - H0)
                act.wait_ge(hid_lo_ready, chunk - 1)
                A.activation(hid[:], silu_g[:], ACT.Square).then_inc(hid_ready, 1)
                act.wait_ge(hid_ready, chunk)
                A.activation(hidden_parts(parts)[0], hid[:], ACT.Copy).then_inc(hid_hi_ready, 1)

            squared(H0 + 1, 0)
            with act.Fori(0, (UP_CHUNKS - 1) // 3) as i:
                for c3 in range(3):
                    n = Slab(MLP + 1 + 2 * c3, 6, i)
                    split_hi(n + 2)
                    split_hi(n + 3)
                    squared(i * 3 + (H0 + c3 + 2), (c3 + 1) % 3)
            split_hi(Slab(MLP + 2 * UP_CHUNKS + 1))
            act.wait_ge(p_turned, 1)
            A.activation(o_hi[:, 0:2], ps[:, MISC], ACT.Copy).then_inc(p_hi_ready, 1)

            def projection_out():
                for b, bank in enumerate(PROJ_BANKS):
                    if b < 3:
                        act.wait_ge(acc_done, 3 * 6 + b + 1)
                    else:
                        act.wait_ge(slab_done, PLE_PROJ + 1)
                    A.activation(proj[:, 2 * b:2 * b + 2], ps[:, bank], ACT.Copy).then_inc(proj_out, 1)

            raw_input(10, 6, 6, tabB[:, R_PLE:R_PLE + KT], Slab(PLE_PROJ + 2), projection_out)
            split_hi(Slab(PLE_GATE + 2))
            for j in range(4):
                act.wait_ge(gate_scaled, j + 1)
                for o in range(2):
                    t = 2 * j + o
                    last = A.activation(gate[:, o], gate[:, o], ACT.Sigmoid, bias=tabB[:, R_PLE_B + t:R_PLE_B + t + 1])
                last.then_inc(gate_out, 1)
                split_hi(Slab(PLE_GATE + j + 3))
                if j == 3:
                    A.preload_act_table(ACT.Sqrt)
                wait_x(act, 7, j)
                if j >= 2:
                    act.wait_ge(sq_used, 4 * 11 + j - 1)
                A.activation(sq[:, j % 2], xt[:, 2 * j:2 * j + 2], ACT.Square).then_inc(sq_ready, 1)
                if j == 0:
                    act.wait_ge(sq_used, 4 * 11)
                for t in (2 * j, 2 * j + 1):
                    last = A.activation(y[:, t], xt[:, t], ACT.Copy, scale=tabB[:, R_FINAL + t:R_FINAL + t + 1])
                last.then_inc(final_ready, 1)
            act.wait_ge(sq_used, 4 * 12)
            A.activation(rms[:], ps[:, MISC, 0:S], ACT.Sqrt, bias=eps[:, 0:1], scale=1.0 / D).then_inc(rms_ready, 1)
            act.wait_ge(final_turned, 4)
            act.wait_ge(rstd_ready, 12)
            for t in range(ST):
                A.activation(out_tok[:, t, 0:512], ps[:, 4 + 2 * t], ACT.Copy, scale=rstd_tok[:, t:t + 1])\
                    .then_inc(out_act, 1)

        @block.vector
        def _(dve):
            def split_lo(n):
                if n.first >= N_SLABS:
                    return
                dve.wait_ge(slab_hi, n.plus(1))
                V.tensor_tensor(w_lo[:, n.place], raw[:, n.place], w_hi[:, n.place].bitcast(F32),
                                ALU.subtract).then_inc(slab_lo, 1)

            def ada(m, place, count, slot, scalars, fresh, buffer=None, loaded=None):
                buffer = ada_raw[:, place] if buffer is None else buffer
                dve.wait_ge(loaded or ada_loaded[place], count)
                for k in range(2):
                    if fresh and k == 0:
                        V.tensor_scalar(ada_sum[:, slot], buffer[:, k], scalars[k], None, ALU.mult)\
                            .then_inc(ada_acc, 1)
                    else:
                        dve.wait_ge(ada_acc, m * 2 + k)
                        V.scalar_tensor_tensor(out=ada_sum[:, slot], in0=buffer[:, k], scalar=scalars[k],
                                               in1=ada_sum[:, slot], op0=ALU.mult, op1=ALU.add)\
                            .then_inc(ada_acc, 1)

            def c_cols(kp):
                return [c_act[:, 2 * kp + k:2 * kp + k + 1] for k in range(2)]

            def ada_static(m, slot):
                place = (m + 1) % ADA_RING
                if m < 8:
                    buffer, loaded = first_mod_place(m)
                    ada(m, place, 32 if m >= 6 else 16, slot, c_cols(m % 4), m % 4 == 0, buffer, loaded)
                else:
                    ada(m, place, 16 * ((m + 1) // 3 - 2), slot, c_cols(m % 4), m % 4 == 0)

            def mod(g, bank, s):
                V.tensor_tensor(mods[:, g], ps[:, bank, s * KT:(s + 1) * KT], tabA[:, g * KT:(g + 1) * KT], ALU.add)\
                    .then_inc(mod_ready, 1)

            def gain_of(i):
                l, k = i // 4, i % 4
                g = 6 * l + (SC_A, G_A, SC_F, G_F)[k]
                dve.wait_ge(mod_ready, g + 1)
                V.scalar_tensor_tensor(out=gain[:, i], in0=mods[:, g], scalar=1.0 if k % 2 == 0 else 0.0,
                                       in1=tabB[:, R_NORM + i * KT:R_NORM + (i + 1) * KT], op0=ALU.add,
                                       op1=ALU.mult).then_inc(gain_ready, 1)

            def inverse_rms(k):
                dve.wait_ge(rms_ready, k + 1)
                V.reciprocal(rstd[:], rms[:]).then_inc(rstd_ready, 1)
                dve.wait_ge(rstd_ready, k + 1)

            def h_input(k, i, gains, shift, inverted=False):
                if not inverted:
                    inverse_rms(k)

                def low(t):
                    dve.wait_ge(h_hi_ready, 8 * i + t + 1)
                    if shift is None:
                        V.tensor_tensor(h_lo[:, t], y[:, t], h_hi[:, t].bitcast(F32), ALU.subtract)\
                            .then_inc(h_ready, 1)
                    else:
                        V.scalar_tensor_tensor(out=h_lo[:, t], in0=y[:, t], scalar=mods[:, shift, t:t + 1],
                                               in1=h_hi[:, t].bitcast(F32), op0=ALU.add, op1=ALU.subtract)\
                            .then_inc(h_ready, 1)

                for t in range(KT):
                    V.scalar_tensor_tensor(out=y[:, t], in0=xt[:, t], scalar=gains[:, t:t + 1], in1=rstd[:],
                                           op0=ALU.mult, op1=ALU.mult).then_inc(h_norm, 1)
                    if t:
                        low(t - 1)
                low(KT - 1)

            def raw_low(i, t, gains):
                dve.wait_ge(h_hi_ready, 8 * i + t + 1)
                V.scalar_tensor_tensor(out=h_lo[:, t], in0=xt[:, t], scalar=gains[:, t:t + 1],
                                       in1=h_hi[:, t].bitcast(F32), op0=ALU.mult, op1=ALU.subtract)\
                    .then_inc(h_ready, 1)

            rstd_pair = rstd[:].rearrange("p (o s) -> p o s", o=1).to_broadcast([P, 2, S])

            def bank(n):
                return ps[:, n.place].rearrange("p (o s) -> p o s", o=2)

            def bank_done(b, sums, slab):
                if b < 3:
                    dve.wait_ge(acc_done, 3 * sums + b + 1)
                else:
                    dve.wait_ge(slab_done, slab + 1)

            def add_y(k, i):
                inverse_rms(k)
                for b in range(4):
                    pair = slice(2 * b, 2 * b + 2)
                    dve.wait_ge(y_gained, 4 * i + b + 1)
                    V.tensor_tensor(y[:, pair], y[:, pair], rstd_pair, ALU.mult).then_inc(y_scaled, 1)
                    if b > 1:
                        dve.wait_ge(y_scaled, 4 * i + b + 1)
                        V.tensor_tensor(xt[:, pair], xt[:, pair], y[:, pair], ALU.add).then_inc(x_ready, 1)

            def add_acc(sums, banks, slab, i, gains):
                for b in range(4):
                    bank_done(b, sums, slab)
                    V.tensor_tensor(xt[:, 2 * b:2 * b + 2], xt[:, 2 * b:2 * b + 2],
                                    ps[:, banks[b]].rearrange("p (o s) -> p o s", o=2), ALU.add)\
                        .then_inc(x_ready, 1)
                    if b:
                        raw_low(i, 2 * b - 2, gains)
                        raw_low(i, 2 * b - 1, gains)
                raw_low(i, 6, gains)
                raw_low(i, 7, gains)

            V.memset(ones[:], 1.0).then_inc(const_ready, 1)
            V.memset(zeros[:], 0.0).then_inc(const_ready, 1)
            V.memset(eps[:], EPS).then_inc(const_ready, 1)
            dve.wait_ge(tab_turned, 1)
            V.tensor_copy(tabA[:, 0:ROW_C + KT], ps[:, 0, 0:ROW_C + KT]).then_inc(tab_ready, 1)
            dve.wait_ge(rel_turned, 1)
            V.tensor_copy(rel_t[:], ps[0:HEADS, 1, 0:N_BUCKETS]).then_inc(rel_ready, 1)
            dve.wait_ge(c_ready, 1)
            for m in range(8):
                if m == 7:
                    dve.wait_ge(tab_turned, 2)
                    V.tensor_copy(tabB[:], ps[:, 2, 0:P]).then_inc(tab_ready, 1)
                    dve.wait_ge(tab_turned, 3)
                    V.tensor_copy(tabC[:, 0:R_SUBLN + 1], ps[:, 0, 0:R_SUBLN + 1]).then_inc(tab_ready, 1)
                ada_static(m, m // 4)
            inverse_rms(0)
            split_lo(Slab(0))
            dve.wait_ge(ada_reduced, 1)
            dve.wait_ge(tab_ready, 3)
            mod(0, 1, 0)
            dve.wait_ge(ada_reduced, 2)
            mod(1, 0, 1)
            gain_of(0)
            dve.wait_ge(gain_ready, 1)
            h_input(0, 0, gain[:, 0], SH_A, inverted=True)
            split_lo(Slab(1))

            for l in range(DEPTH):
                units = 1 + l

                def biased(pairs, h0):
                    dve.wait_ge(s_done, pairs)
                    if l == 0:
                        V.tensor_tensor(prob[:, 0:2, 0:S], ps[:, 4].rearrange("p (h s) -> p h s", h=2),
                                        bias[:, ds(h0, 2), 0:S], ALU.add)
                        last = V.tensor_tensor(prob[:, 0:2, S:S + P], ps[:, 5, 0:S].rearrange("p (h s) -> p h s", h=2),
                                               bias[:, ds(h0, 2), S:S + P], ALU.add)
                    else:
                        for hh in range(2):
                            for cc in range(2):
                                V.tensor_tensor(prob[:, 2 * hh + cc:2 * hh + cc + 1, 0:S],
                                                ps[:, 4 + cc:5 + cc, hh * S:(hh + 1) * S],
                                                bias[:, ds(h0 + hh, 1), 0:S], ALU.add)
                                u, b = 2 * hh + cc, 6 + cc
                                last = V.tensor_tensor(prob[:, u:u + 1, S:S + P], ps[:, b:b + 1, hh * P:(hh + 1) * P],
                                                       bias[:, ds(h0 + hh, 1), S:S + P], ALU.add)
                    last.then_inc(s_biased, 1)
                    dve.wait_ge(s_biased, pairs)
                    U = 2 * units
                    V.tensor_reduce(sums[:, 0, 0:U], prob[:, 0:U, 0:S], AX_X, ALU.max)
                    V.tensor_reduce(sums[:, 1, 0:U], prob[:, 0:U, S:S + P], AX_X, ALU.max).then_inc(s_max, 1)
                    dve.wait_ge(s_max, pairs)
                    V.tensor_scalar(maxes[:, :, 0:U], sums[:, :, 0:U], -1.0, None, ALU.mult).then_inc(s_negmax, 1)

                def normalised(pairs, j):
                    U = 2 * units
                    dve.wait_ge(s_exp, pairs)
                    V.reciprocal(rsums[:, :, 0:U], sums[:, :, 0:U]).then_inc(s_rsum, 1)
                    dve.wait_ge(s_rsum, pairs)
                    if l == 0:
                        for u in range(2):
                            for part, at in ((0, slice(0, S)), (1, slice(S, S + P))):
                                last = V.tensor_scalar(prob[:, u, at], prob[:, u, at], rsums[:, part, u:u + 1],
                                                       None, ALU.mult)
                        last.then_inc(p_ready, 1)
                        return
                    V.tensor_scalar(rsums[:, :, 1:4:2], rsums[:, :, 1:4:2], neg_lam[:, 0:1], None, ALU.mult)\
                        .then_inc(s_mixed, 1)
                    dve.wait_ge(s_mixed, j * 2 - 1)
                    for hh in range(2):
                        for part, at in ((0, slice(0, S)), (1, slice(S, S + P))):
                            u = 2 * hh + 1
                            last = V.tensor_scalar(prob[:, u, at], prob[:, u, at], rsums[:, part, u:u + 1],
                                                   None, ALU.mult)
                    last.then_inc(s_mixed, 1)
                    dve.wait_ge(s_mixed, j * 2)
                    for hh in range(2):
                        for part, at in ((0, slice(0, S)), (1, slice(S, S + P))):
                            u = 2 * hh
                            last = V.scalar_tensor_tensor(out=prob[:, u, at], in0=prob[:, u, at],
                                                          scalar=rsums[:, part, u:u + 1], in1=prob[:, u + 1, at],
                                                          op0=ALU.mult, op1=ALU.add)
                    last.then_inc(p_ready, 1)

                def heads_low(pairs, at):
                    dve.wait_ge(o_hi_ready, pairs)
                    if l == 0:
                        V.tensor_tensor(o_lo[:, at], ps[:, MISC].rearrange("p (h s) -> p h s", h=2),
                                        o_hi[:, at].bitcast(F32), ALU.subtract).then_inc(o_ready, 1)
                    else:
                        V.tensor_tensor(o_lo[:, at], hid[:], o_hi[:, at].bitcast(F32), ALU.subtract)\
                            .then_inc(o_ready, 1)

                def heads_normalised(j):
                    dve.wait_ge(head_rms, j)
                    V.reciprocal(sq[:, 1], sq[:, 0]).then_inc(head_rstd, 1)
                    dve.wait_ge(head_rstd, j)
                    V.scalar_tensor_tensor(out=hid[:], in0=hid[:], scalar=subln[:, 0:1], in1=sq[:, 1],
                                           op0=ALU.mult, op1=ALU.mult).then_inc(head_norm, 1)

                def pair(j, n, first):
                    pairs = j + PAIRS * l
                    split_lo(n + 2)
                    V.tensor_copy(c_pair[:], c_act[:, ds(2 * j, 2)]).then_inc(c_pair_ready, 1)
                    dve.wait_ge(c_pair_ready, pairs + 1)
                    cs = [c_pair[:, k:k + 1] for k in range(2)]

                    def step_ada(c3):
                        if l == 0:
                            ada(j * 3 + (8 + c3), c3, j * 16 + 16, c3, cs, first)
                        elif c3 == 0:
                            ada(j + 44, 2, j * 16 + 16 * 6, 0, cs, first)
                    step_ada(0)
                    split_lo(n + 3)
                    step_ada(1)
                    split_lo(n + 4)
                    if l == 0 and not first:
                        heads_low(pairs, ds(2 * j - 2, 2))
                    if l == 0 and first:
                        dve.wait_ge(bias_ready, 6)
                    biased(pairs + 1, 2 * j)
                    if l and not first:
                        heads_normalised(j)
                    step_ada(2)
                    normalised(pairs + 1, j + 1)
                    if l and not first:
                        heads_low(pairs, ds(2 * j - 2, 2))

                pair(0, Slab(ATTN[l]), True)
                with dve.Fori(1, PAIRS) as j:
                    pair(j, Slab(ATTN[l], 3, j), False)
                pairs = PAIRS * (l + 1)
                n = Slab(OPROJ[l])
                split_lo(n + 2)
                split_lo(n + 3)
                if l:
                    heads_normalised(PAIRS)
                heads_low(pairs, slice(6, 8))
                split_lo(n + 4)
                dve.wait_ge(ada_reduced, 3 if l == 0 else 10)
                if l == 0:
                    for s in range(3):
                        mod(G_A + s, 5, s)
                    gain_of(1)
                    gain_of(2)
                    ada_static(20, 0)
                    ada_static(21, 0)
                    ada_static(22, 0)
                else:
                    mod(11, 5, 0)
                    gain_of(7)
                split_lo(n + 5)
                dve.wait_ge(gain_ready, 3 if l == 0 else 8)
                add_y(1 + 4 * l, 2 * l)
                h_input(2 + 4 * l, 2 * l + 1, gain[:, 4 * l + 2], 6 * l + SH_F)

                def hidden(n, chunk):
                    dve.wait_ge(silu_ready, chunk)
                    dve.wait_ge(slab_done, n.plus(2))
                    if not isinstance(chunk, int) or chunk > 1:
                        dve.wait_ge(hid_lo_ready, chunk - 1)
                    V.tensor_tensor(hid[:], silu_g[:], ps[:, (n + 1).place].rearrange("p (o s) -> p o s", o=2),
                                    ALU.mult).then_inc(hid_ready, 1)

                def hidden_lo(chunk, parts):
                    hi, lo = hidden_parts(parts)
                    dve.wait_ge(hid_hi_ready, chunk)
                    V.tensor_tensor(lo, hid[:], hi.bitcast(F32), ALU.subtract)\
                        .then_inc(hid_lo_ready, 1)

                n = Slab(FFN[l])
                split_lo(n + 2)
                if l == 0:
                    ada_static(23, 0)
                split_lo(n + 3)
                hidden(n, FF_CHUNKS * l + 1)
                hidden_lo(FF_CHUNKS * l + 1, 0)
                if l == 0:
                    dve.wait_ge(ada_reduced, 4)
                    mod(G_F, MISC, 0)
                    gain_of(3)
                with dve.Fori(0, (FF_CHUNKS - 1) // 2) as i:
                    for c2 in range(2):
                        n = Slab(FFN[l] + 2 + 3 * c2, 6, i)
                        chunk = i * 2 + (FF_CHUNKS * l + c2 + 2)

                        def step_ada(kp):
                            ada(i * 4 + (24 + kp), (kp + 1) % 2, i * 32 + 16 * (6 + kp // 2 + kp % 2), 0,
                                c_cols(kp), kp == 0)

                        split_lo(n + 2)
                        if l == 0:
                            step_ada((0, 3)[c2])
                        split_lo(n + 3)
                        if l == 0 and c2 == 0:
                            step_ada(1)
                        if l == 0 and c2 == 1:
                            dve.wait_ge(ada_hi_ready, i + 1)
                            V.tensor_tensor(ada_lo, ada_sum[:, 0], ada_hi.bitcast(F32), ALU.subtract)\
                                .then_inc(ada_lo_ready, 1)
                        hidden(n, chunk)
                        split_lo(n + 4)
                        if l == 0 and c2 == 0:
                            step_ada(2)
                        hidden_lo(chunk, 1 - c2)
                        if l == 0 and c2 == 1:
                            dve.wait_ge(ada_reduced, i + 5)
                            V.tensor_tensor(mods[:, ds(i + 6, 1)], ps[:, MISC:MISC + 1, 0:2 * KT:2],
                                            tabA[:, ds(i * KT + 6 * KT, KT)].rearrange("p (a b) -> p a b", a=1),
                                            ALU.add).then_inc(mod_ready, 1)
                split_lo(Slab(FFN[l] + 3 * FF_CHUNKS + 1))
                if l == 0:
                    for i in (4, 5, 6):
                        gain_of(i)
                    dve.wait_ge(lam_loaded, 16)
                    V.tensor_tensor(lam_prod[:], lam_in[:, 0:4:2], lam_in[:, 1:4:2], ALU.mult).then_inc(lam_step, 1)
                    V.tensor_scalar(lruc[:, 0], tabC[:, R_L:R_L + CT], -1.0, None, ALU.mult).then_inc(lruc_step, 1)
                    V.tensor_scalar(subln[:], tabC[:, R_SUBLN:R_SUBLN + 1], 1.0 - LAMBDA_INIT, None, ALU.mult)
                    dve.wait_ge(lam_step, 1)
                    V.tensor_reduce(lam_s[:, 0:2], lam_prod[:], AX_X, ALU.add).then_inc(lam_step, 1)
                    dve.wait_ge(lruc_step, 1)
                    V.tensor_tensor(lruc[:, 1], tabC[:, R_L:R_L + CT], lruc[:, 0], ALU.min).then_inc(lruc_step, 1)
                    dve.wait_ge(gain_ready, 7)
                add_y(3 + 4 * l, 2 * l + 1)
                if l == 0:
                    h_input(4, 2, gain[:, 4], 6 + SH_A)
                    dve.wait_ge(lam_exp, 1)
                    V.tensor_tensor(lam_s[:, 0:1], lam_s[:, 3:4], lam_s[:, 2:3], ALU.subtract).then_inc(lam_step, 1)
                    dve.wait_ge(lam_step, 3)
                    V.tensor_scalar(neg_lam[:], lam_s[:, 0:1], -LAMBDA_INIT, None, ALU.add).then_inc(lam_step, 1)
                    dve.wait_ge(lam_step, 4)
                    dve.wait_ge(lruc_exp, 1)
                    done = [2]

                    def step(ins):
                        done[0] += 1
                        ins.then_inc(lruc_step, 1)
                        dve.wait_ge(lruc_step, done[0])

                    u, s1, s2, q = lruc[:, 2], lruc[:, 3], lruc[:, 4], lruc[:, 5]
                    step(V.tensor_scalar(s1, u, 2.0, None, ALU.add))
                    step(V.reciprocal(s1, s1))
                    step(V.tensor_tensor(s1, s1, u, ALU.mult))
                    step(V.tensor_tensor(s2, s1, s1, ALU.mult))
                    step(V.tensor_scalar(q, s2, 1.0 / 17, None, ALU.mult))
                    for m in range(7, 0, -1):
                        step(V.scalar_tensor_tensor(out=q, in0=q, scalar=1.0 / (2 * m + 1), in1=s2, op0=ALU.add,
                                                    op1=ALU.mult))
                    step(V.scalar_tensor_tensor(out=q, in0=q, scalar=1.0, in1=s1, op0=ALU.add, op1=ALU.mult))
                    step(V.tensor_scalar(lruc[:, 6], tabC[:, R_L:R_L + CT], 0.0, LRU_C, ALU.min, ALU.mult))
                    step(V.scalar_tensor_tensor(out=lruc[:, 7], in0=q, scalar=-2.0 * LRU_C, in1=lruc[:, 6],
                                                op0=ALU.mult, op1=ALU.add))
                    assert done[0] == LRUC_STEPS
                else:
                    for t in range(KT):
                        raw_low(4, t, tabB[:, R_MIX:R_MIX + KT])

            n = Slab(MIX_IN)
            V.memset(ul[:, :, 0:PADC], 0.0).then_inc(pads_zero, 1)
            V.memset(win[0][:, :, 0:PADW], 0.0)
            V.memset(win[1][:, :, 0:PADW], 0.0).then_inc(pads_zero, 1)

            def branch(s, dst):
                dve.wait_ge(slab_done, MIX_IN + s + 1)
                V.tensor_tensor(dst, bank(n + s), rstd_pair, ALU.mult).then_inc(mix_out, 1)

            split_lo(n + 2)
            inverse_rms(8)
            V.memset(up[:, :, 0:PADW], 0.0).then_inc(pads_zero, 1)

            def conv(t0, steps):
                for k in range(CONV):
                    for t in (t0, t0 + 1):
                        w = tabB[:, R_CONV_W + k * CT + t:R_CONV_W + k * CT + t + 1]
                        if k == 0:
                            last = V.tensor_scalar(xb[:, t], ul[:, t, 0:S], w, tabB[:, R_CONV_B + t:R_CONV_B + t + 1],
                                                   ALU.mult, ALU.add)
                        else:
                            last = V.scalar_tensor_tensor(out=xb[:, t], in0=ul[:, t, k:k + S], scalar=w,
                                                          in1=xb[:, t], op0=ALU.mult, op1=ALU.add)
                        last.then_inc(conv_step, 1)
                    if k < CONV - 1:
                        dve.wait_ge(conv_step, steps + 2 * k + 2)

            branch(0, ul[:, 0:2, PADC:PADC + S])
            split_lo(n + 3)
            branch(1, ul[:, 2:4, PADC:PADC + S])
            dve.wait_ge(pads_zero, 3)
            dve.wait_ge(mix_out, 2)
            conv(0, 0)
            conv(2, 2 * CONV)
            split_lo(n + 4)
            split_lo(n + 5)
            branch(2, up[:, 0:2, PADW:PADW + S])
            branch(3, up[:, 2:4, PADW:PADW + S])
            dve.wait_ge(mix_out, 4)
            src = up
            for g in range(len(POOL_WINDOWS)):
                dst, lag = win[g % 2], 1 << g
                V.tensor_tensor(dst[:, g:CT, PADW:], src[:, g:CT, PADW:], src[:, g:CT, PADW - lag:PADW - lag + S],
                                ALU.add).then_inc(pool_step, 1)
                dve.wait_ge(pool_step, g + 1)
                src = dst
            dve.wait_ge(inv_ready, 1)
            for g, w in enumerate(POOL_WINDOWS):
                V.scalar_tensor_tensor(out=pool_d[:, g, w:S], in0=win[g % 2][:, g, PADW + w:], scalar=1.0 / w,
                                       in1=up[:, g, PADW + w:], op0=ALU.mult, op1=ALU.subtract)
            for g, w in enumerate(POOL_WINDOWS):
                last = V.tensor_tensor(pool_d[:, g, 0:w], win[g % 2][:, g, PADW:PADW + w], inv_t[:, 0:w], ALU.mult)
            last.then_inc(pool_step, 1)
            dve.wait_ge(pool_step, 5)
            for g, w in enumerate(POOL_WINDOWS):
                last = V.tensor_tensor(pool_d[:, g, 0:w], pool_d[:, g, 0:w], up[:, g, PADW:PADW + w], ALU.subtract)
            last.then_inc(pool_done, 1)
            dve.wait_ge(gates_out, 4)
            V.tensor_tensor(gate_i[:], gate_i[:], xb[:], ALU.mult).then_inc(lru_in, 1)
            split_lo(n + 6)
            dve.wait_ge(lru_exp, 1)
            V.tensor_tensor(mult[:], a_t[:], a_t[:], ALU.mult).then_inc(lru_step, 1)
            dve.wait_ge(lru_step, 1)
            V.scalar_tensor_tensor(out=th[:], in0=mult[:], scalar=1.0, in1=th[:], op0=ALU.add, op1=ALU.mult)\
                .then_inc(lru_step, 1)
            dve.wait_ge(pool_mm, 1)
            for t in range(CT):
                last = V.tensor_scalar(pool_d[:, t], ps[:, 4 + t // 2, (t % 2) * S:(t % 2) * S + S],
                                       tabC[:, R_POOL_B + t:R_POOL_B + t + 1], tabC[:, R_POOL_S + t:R_POOL_S + t + 1],
                                       ALU.add, ALU.mult)
            last.then_inc(pool_out, 1)
            branch(4, gelu_t[:, 0:2])
            dve.wait_ge(lru_mult, 1)
            V.memset(mult[:, :, 0:1], 1.0).then_inc(lru_in, 1)
            dve.wait_ge(lru_in, 2)
            V.tensor_tensor(gate_i[:], gate_i[:], mult[:], ALU.mult).then_inc(lru_in, 1)
            dve.wait_ge(mix_hi, 1)
            V.tensor_tensor(o_lo[:, 0:CT], pool_d[:], o_hi[:, 0:CT].bitcast(F32), ALU.subtract).then_inc(mix_ready, 1)
            dve.wait_ge(lru_in, 3)
            for t in range(CT):
                last = V.tensor_tensor_scan(lru_h[:, t], a_t[:, t], gate_i[:, t], 0.0, ALU.mult, ALU.add)
            last.then_inc(lru_scan, 1)
            split_lo(n + 7)
            branch(5, gelu_t[:, 2:4])
            dve.wait_ge(gelu_ready, 2)
            dve.wait_ge(lru_scan, 1)
            V.tensor_tensor(lru_h[:], lru_h[:], gelu_t[:], ALU.mult).then_inc(lru_ready, 1)
            split_lo(n + 8)
            dve.wait_ge(mix_hi, 2)
            V.tensor_tensor(o_lo[:, CT:2 * CT], lru_h[:], o_hi[:, CT:2 * CT].bitcast(F32), ALU.subtract)\
                .then_inc(mix_ready, 1)
            split_lo(n + 9)
            split_lo(n + 10)
            split_lo(n + 11)
            add_acc(4, FF_ACC, MIX_OUT + 3, 5, tabB[:, R_MLP:R_MLP + KT])

            H0 = DEPTH * FF_CHUNKS

            def rectified(n, chunk):
                dve.wait_ge(slab_done, n.plus(1))
                dve.wait_ge(hid_ready, chunk - 1)
                V.scalar_tensor_tensor(out=silu_g[:], in0=bank(n), scalar=0.0, in1=rstd_pair, op0=ALU.max,
                                       op1=ALU.mult).then_inc(relu_ready, 1)

            def squared_lo(chunk, parts):
                hi, lo = hidden_parts(parts)
                dve.wait_ge(hid_hi_ready, chunk)
                V.tensor_tensor(lo, hid[:], hi.bitcast(F32), ALU.subtract).then_inc(hid_lo_ready, 1)

            n = Slab(MLP)
            split_lo(n + 2)
            inverse_rms(9)
            rectified(n, H0 + 1)
            squared_lo(H0 + 1, 0)
            with dve.Fori(0, (UP_CHUNKS - 1) // 3) as i:
                for c3 in range(3):
                    n = Slab(MLP + 1 + 2 * c3, 6, i)
                    split_lo(n + 2)
                    rectified(n, i * 3 + (H0 + c3 + 2))
                    split_lo(n + 3)
                    squared_lo(i * 3 + (H0 + c3 + 2), (c3 + 1) % 3)
            split_lo(Slab(MLP + 2 * UP_CHUNKS + 1))
            dve.wait_ge(p_hi_ready, 1)
            V.tensor_tensor(o_lo[:, 0:2], ps[:, MISC].rearrange("p (o s) -> p o s", o=2), o_hi[:, 0:2].bitcast(F32),
                            ALU.subtract).then_inc(p_lo_ready, 1)
            add_acc(5, FF_ACC, MLP + 2 * UP_CHUNKS - 1, 6, tabB[:, R_PLE:R_PLE + KT])
            split_lo(Slab(PLE_PROJ + 2))
            inverse_rms(10)
            split_lo(Slab(PLE_GATE + 2))
            dve.wait_ge(proj_out, 4)
            for j in range(4):
                js = slice(2 * j, 2 * j + 2)
                dve.wait_ge(slab_done, PLE_GATE + j + 1)
                if j:
                    dve.wait_ge(gate_mixed, j)
                V.tensor_tensor(gate[:], bank(Slab(PLE_GATE + j)), rstd_pair, ALU.mult).then_inc(gate_scaled, 1)
                dve.wait_ge(gate_out, j + 1)
                V.tensor_tensor(proj[:, js], gate[:], proj[:, js], ALU.mult).then_inc(gate_mixed, 1)
                dve.wait_ge(gate_mixed, j + 1)
                V.tensor_tensor(xt[:, js], xt[:, js], proj[:, js], ALU.add).then_inc(x_ready, 1)
                split_lo(Slab(PLE_GATE + j + 3))
            dve.wait_ge(rms_turned, 1)
            V.reciprocal(rstd_tok[:], ps[:, MISC, S:S + ST]).then_inc(rstd_ready, 1)
            dve.wait_ge(rstd_ready, 12)
            for t in range(ST):
                V.tensor_scalar(out_tok[:, t, 512:1024], ps[:, 5 + 2 * t], rstd_tok[:, t:t + 1], None, ALU.mult)\
                    .then_inc(out_dve, 1)


_INS = ['x', 'c', 'rel_bias', 'ada_w', 'ada_b', 'norm_g', 'moba_w_qkv', 'moba_w_o', 'diff_w_qkv', 'diff_w_o',
        'diff_lambda', 'diff_subln_g', 'ffn_w_in', 'ffn_w_out', 'p_2', 'norm_mix_g_2', 'w_in_2', 'pool_w_2',
        'pool_b_2', 'pool_scale_2', 'conv_w_2', 'conv_b_2', 'gate_a_w_2', 'gate_a_b_2', 'gate_x_w_2',
        'gate_x_b_2', 'lru_L_2', 'w_out_2', 'norm_mlp_g_2', 'w_up_2', 'w_down_2', 'norm_ple_g_2',
        'w_ple_gate_2', 'b_ple_gate_2', 'w_ple_proj_2', 'norm_final_g_2']


def kernel(**inputs):
    import concourse.bacc as bacc
    from concourse.bass_utils import run_bass_kernel_spmd

    nc = bacc.Bacc("TRN2", target_bir_lowering=False, num_devices=1)
    arrays, args = {}, []
    for name in _INS:
        a = np.ascontiguousarray(inputs[name])
        arrays[f"in_{name}"] = a
        args.append(nc.dram_tensor(f"in_{name}", a.shape, mybir.dt.from_np(a.dtype), kind="ExternalInput").ap())
    args.append(nc.dram_tensor("out_x", (1, S, D), F32, kind="ExternalOutput").ap())
    build(nc, *args)
    return run_bass_kernel_spmd(nc, [arrays], core_ids=[0]).results[0]["out_x"]
```
